# Optimizing a Trainium2 kernel written in Bass

```python
import jax, jax.numpy as jnp
from jax import lax
import numpy as np

D_MODEL = 1024
BATCH = 1
SEQ = 256
DEPTH = 1

N_MEM = 256
EPS = 1e-6
FOX_HEADS = 8
FOX_HEAD_DIM = 64
FOX_WIDTH = FOX_HEADS * FOX_HEAD_DIM
Q_BLOCK = 128
GDN_HEADS = 4
GDN_HEAD_DIM = 128
GDN_WIDTH = GDN_HEADS * GDN_HEAD_DIM
CONV_WIDTH = 4
CHUNK = 64
MIX_WIDTH = FOX_WIDTH + GDN_WIDTH
IN_PROJ_SIZES = (FOX_WIDTH, FOX_WIDTH, FOX_WIDTH, FOX_HEADS,
                 GDN_WIDTH, GDN_WIDTH, GDN_WIDTH, GDN_WIDTH, GDN_HEADS, GDN_HEADS)
IN_PROJ_WIDTH = sum(IN_PROJ_SIZES)
SPLIT_POINTS = tuple(np.cumsum(IN_PROJ_SIZES)[:-1].tolist())
MEM_HEADS = 4
MEM_HEAD_DIM = D_MODEL // MEM_HEADS
D_FF = 2816
FFN_RESIDUAL_WEIGHT = 0.5


def rms_norm(x, gain):
    xf = x.astype(jnp.float32)
    y = xf * lax.rsqrt(jnp.mean(xf * xf, axis=-1, keepdims=True) + EPS)
    return (y * gain.astype(jnp.float32)).astype(x.dtype)

def l2_norm(x):
    return x * lax.rsqrt(jnp.sum(x * x, axis=-1, keepdims=True) + EPS)

def swiglu(x, w_gate, w_up, w_down):
    return (jax.nn.silu(x @ w_gate) * (x @ w_up)) @ w_down

def forgetting_attention(q, k, v, f_logit):
    B, S, H, Dh = q.shape
    nb = S // Q_BLOCK
    F = jnp.cumsum(jax.nn.log_sigmoid(f_logit.astype(jnp.float32)), axis=1).transpose(0, 2, 1)
    qb = (q * (Dh ** -0.5)).reshape(B, nb, Q_BLOCK, H, Dh).transpose(1, 0, 3, 2, 4)
    Fq = F.reshape(B, H, nb, Q_BLOCK).transpose(2, 0, 1, 3)
    q_pos = jnp.arange(S).reshape(nb, Q_BLOCK)
    k_pos = jnp.arange(S)

    def block(args):
        q_blk, F_blk, pos_blk = args
        s = jnp.einsum('bhqd,bshd->bhqs', q_blk, k, preferred_element_type=jnp.float32)
        s = s + F_blk[..., None] - F[:, :, None, :]
        s = jnp.where(pos_blk[:, None] >= k_pos[None, :], s, -jnp.inf)
        p = jax.nn.softmax(s, axis=-1).astype(v.dtype)
        return jnp.einsum('bhqs,bshd->bqhd', p, v)

    out = lax.map(block, (qb, Fq, q_pos))
    return out.transpose(1, 0, 2, 3, 4).reshape(B, S, H * Dh)

def causal_conv_silu(x, w):
    S = x.shape[1]
    xp = jnp.pad(x, ((0, 0), (CONV_WIDTH - 1, 0), (0, 0)))
    y = xp[:, 0:S] * w[0]
    for i in range(1, CONV_WIDTH):
        y = y + xp[:, i:i + S] * w[i]
    return jax.nn.silu(y)

def gated_delta_rule_chunked(q, k, v, g, beta):
    B, S, H, Dk = q.shape
    Dv = v.shape[-1]
    n = S // CHUNK

    def chunks(t):
        return t.reshape(B, n, CHUNK, H, -1).transpose(0, 3, 1, 2, 4)

    q = chunks(q) * (Dk ** -0.5)
    k = chunks(k)
    v = chunks(v)
    beta = beta.reshape(B, n, CHUNK, H).transpose(0, 3, 1, 2)
    g = jnp.cumsum(g.reshape(B, n, CHUNK, H).transpose(0, 3, 1, 2), axis=-1)
    k_beta = k * beta[..., None]
    v_beta = v * beta[..., None]
    incl = jnp.tril(jnp.ones((CHUNK, CHUNK), dtype=bool))
    strict = jnp.tril(jnp.ones((CHUNK, CHUNK), dtype=bool), -1)
    decay = jnp.exp(jnp.where(incl, g[..., :, None] - g[..., None, :], -jnp.inf))
    L = jnp.where(strict, jnp.einsum('bhncd,bhnsd->bhncs', k_beta, k) * decay, 0.0)
    A = L + jnp.eye(CHUNK, dtype=L.dtype)
    u = lax.linalg.triangular_solve(A, v_beta, left_side=True, lower=True)
    w = lax.linalg.triangular_solve(A, k_beta * jnp.exp(g)[..., None], left_side=True, lower=True)
    attn_intra = jnp.einsum('bhncd,bhnsd->bhncs', q, k) * decay
    q_decay = q * jnp.exp(g)[..., None]
    g_last = g[..., -1]
    k_tail = k * jnp.exp(g_last[..., None] - g)[..., None]

    def step(state, xs):
        w_c, u_c, qd_c, a_c, kt_c, gl_c = xs
        v_new = u_c - jnp.einsum('bhcd,bhde->bhce', w_c, state)
        o = jnp.einsum('bhcd,bhde->bhce', qd_c, state) + jnp.einsum('bhcs,bhse->bhce', a_c, v_new)
        state = state * jnp.exp(gl_c)[..., None, None] + jnp.einsum('bhcd,bhce->bhde', kt_c, v_new)
        return state, o

    xs = (jnp.moveaxis(w, 2, 0), jnp.moveaxis(u, 2, 0), jnp.moveaxis(q_decay, 2, 0),
          jnp.moveaxis(attn_intra, 2, 0), jnp.moveaxis(k_tail, 2, 0), jnp.moveaxis(g_last, 2, 0))
    state0 = jnp.zeros((B, H, Dk, Dv), jnp.float32)
    _, o = lax.scan(step, state0, xs)
    return o.transpose(1, 0, 3, 2, 4).reshape(B, S, H, Dv)

def hybrid_mixer(u, w_in, fox_f_bias, gdn_conv_w, gdn_a_log, gdn_dt_bias, gdn_out_norm):
    B, S, _ = u.shape
    proj = u @ w_in
    fq, fk, fv, ff, gq, gk, gv, gz, gb, ga = jnp.split(proj, SPLIT_POINTS, axis=-1)
    fox = forgetting_attention(fq.reshape(B, S, FOX_HEADS, FOX_HEAD_DIM),
                               fk.reshape(B, S, FOX_HEADS, FOX_HEAD_DIM),
                               fv.reshape(B, S, FOX_HEADS, FOX_HEAD_DIM),
                               ff + fox_f_bias)
    qkv = causal_conv_silu(jnp.concatenate([gq, gk, gv], axis=-1).astype(jnp.float32),
                           gdn_conv_w.astype(jnp.float32))
    cq, ck, cv = jnp.split(qkv, (GDN_WIDTH, 2 * GDN_WIDTH), axis=-1)
    q = l2_norm(cq.reshape(B, S, GDN_HEADS, GDN_HEAD_DIM))
    k = l2_norm(ck.reshape(B, S, GDN_HEADS, GDN_HEAD_DIM))
    v = cv.reshape(B, S, GDN_HEADS, GDN_HEAD_DIM)
    beta = jax.nn.sigmoid(gb.astype(jnp.float32))
    g = -jnp.exp(gdn_a_log.astype(jnp.float32)) * jax.nn.softplus(
        ga.astype(jnp.float32) + gdn_dt_bias.astype(jnp.float32))
    o = gated_delta_rule_chunked(q, k, v, g, beta)
    o = rms_norm(o, gdn_out_norm) * jax.nn.silu(
        gz.astype(jnp.float32).reshape(B, S, GDN_HEADS, GDN_HEAD_DIM))
    gdn = o.reshape(B, S, GDN_WIDTH).astype(u.dtype)
    return jnp.concatenate([fox.astype(u.dtype), gdn], axis=-1)

def memory_cross_attention(h, m, w_q, w_kv, w_o):
    B, S, _ = h.shape
    q = (h @ w_q).reshape(B, S, MEM_HEADS, MEM_HEAD_DIM)
    k, v = jnp.split(m @ w_kv, 2, axis=-1)
    k = k.reshape(B, -1, MEM_HEADS, MEM_HEAD_DIM)
    v = v.reshape(B, -1, MEM_HEADS, MEM_HEAD_DIM)
    s = jnp.einsum('bqhd,bmhd->bhqm', q, k, preferred_element_type=jnp.float32) * (MEM_HEAD_DIM ** -0.5)
    p = jax.nn.softmax(s, axis=-1).astype(v.dtype)
    o = jnp.einsum('bhqm,bmhd->bqhd', p, v).reshape(B, S, D_MODEL)
    return o @ w_o

def first_inputs(seed: int = 0) -> dict:
    key = jax.random.key(seed)
    ks = iter(jax.random.split(key, 40))

    def normal(shape, scale):
        return jax.random.normal(next(ks), shape, jnp.float32) * scale

    def gain(width):
        return 1.0 + normal((DEPTH, width), 0.02)

    L = DEPTH
    dt = jnp.exp(jax.random.uniform(next(ks), (L, GDN_HEADS), jnp.float32,
                                    minval=float(np.log(1e-3)), maxval=float(np.log(1e-1))))
    return {
        'x': normal((BATCH, SEQ, D_MODEL), 1.0),
        'mem': normal((BATCH, N_MEM, D_MODEL), 1.0),
        'ffn1_pre_norm': gain(D_MODEL),
        'ffn1_w_gate': normal((L, D_MODEL, D_FF), D_MODEL ** -0.5),
        'ffn1_w_up': normal((L, D_MODEL, D_FF), D_MODEL ** -0.5),
        'ffn1_w_down': normal((L, D_FF, D_MODEL), D_FF ** -0.5),
        'ffn1_post_norm': gain(D_MODEL),
        'mix_pre_norm': gain(D_MODEL),
        'w_in': normal((L, D_MODEL, IN_PROJ_WIDTH), D_MODEL ** -0.5),
        'fox_f_bias': jax.random.uniform(next(ks), (L, FOX_HEADS), jnp.float32, minval=1.0, maxval=4.0),
        'gdn_conv_w': normal((L, CONV_WIDTH, 3 * GDN_WIDTH), CONV_WIDTH ** -0.5),
        'gdn_a_log': jnp.log(jax.random.uniform(next(ks), (L, GDN_HEADS), jnp.float32, minval=1.0, maxval=16.0)),
        'gdn_dt_bias': dt + jnp.log(-jnp.expm1(-dt)),
        'gdn_out_norm': gain(GDN_HEAD_DIM),
        'w_out': normal((L, MIX_WIDTH, D_MODEL), MIX_WIDTH ** -0.5),
        'mix_post_norm': gain(D_MODEL),
        'mem_pre_norm': gain(D_MODEL),
        'mem_kv_norm': gain(D_MODEL),
        'mem_w_q': normal((L, D_MODEL, D_MODEL), D_MODEL ** -0.5),
        'mem_w_kv': normal((L, D_MODEL, 2 * D_MODEL), D_MODEL ** -0.5),
        'mem_w_o': normal((L, D_MODEL, D_MODEL), D_MODEL ** -0.5),
        'mem_post_norm': gain(D_MODEL),
        'ffn2_pre_norm': gain(D_MODEL),
        'ffn2_w_gate': normal((L, D_MODEL, D_FF), D_MODEL ** -0.5),
        'ffn2_w_up': normal((L, D_MODEL, D_FF), D_MODEL ** -0.5),
        'ffn2_w_down': normal((L, D_FF, D_MODEL), D_FF ** -0.5),
        'ffn2_post_norm': gain(D_MODEL),
    }

def first_block(x, mem, ffn1_pre_norm, ffn1_w_gate, ffn1_w_up, ffn1_w_down, ffn1_post_norm,
              mix_pre_norm, w_in, fox_f_bias, gdn_conv_w, gdn_a_log, gdn_dt_bias, gdn_out_norm,
              w_out, mix_post_norm, mem_pre_norm, mem_kv_norm, mem_w_q, mem_w_kv, mem_w_o,
              mem_post_norm, ffn2_pre_norm, ffn2_w_gate, ffn2_w_up, ffn2_w_down, ffn2_post_norm):
    h = x
    for l in range(DEPTH):
        f = swiglu(rms_norm(h, ffn1_pre_norm[l]), ffn1_w_gate[l], ffn1_w_up[l], ffn1_w_down[l])
        h = h + FFN_RESIDUAL_WEIGHT * rms_norm(f, ffn1_post_norm[l])
        mixed = hybrid_mixer(rms_norm(h, mix_pre_norm[l]), w_in[l], fox_f_bias[l], gdn_conv_w[l],
                             gdn_a_log[l], gdn_dt_bias[l], gdn_out_norm[l])
        h = h + rms_norm(mixed @ w_out[l], mix_post_norm[l])
        c = memory_cross_attention(rms_norm(h, mem_pre_norm[l]), rms_norm(mem, mem_kv_norm[l]),
                                   mem_w_q[l], mem_w_kv[l], mem_w_o[l])
        h = h + rms_norm(c, mem_post_norm[l])
        f = swiglu(rms_norm(h, ffn2_pre_norm[l]), ffn2_w_gate[l], ffn2_w_up[l], ffn2_w_down[l])
        h = h + FFN_RESIDUAL_WEIGHT * rms_norm(f, ffn2_post_norm[l])
    return h


DEPTH_2 = 2

PLE_DIM = 256
SC_WIDTH = D_MODEL
SC_KERNEL = 3
SSM_INNER = 2 * D_MODEL
SSM_HEADDIM = 64
SSM_HEADS = SSM_INNER // SSM_HEADDIM
SSM_GROUPS = 4
SSM_STATE = 128
SSM_CONV = 4
SSM_CHUNK = 128
SSM_CONV_DIM = SSM_INNER + 2 * SSM_GROUPS * SSM_STATE
PROJ_SIZES = (SC_WIDTH, SC_WIDTH, SC_WIDTH,
              SSM_INNER, SSM_CONV_DIM, SSM_HEADS,
              D_MODEL, D_MODEL)
PROJ_DIM = sum(PROJ_SIZES)
PROJ_SPLITS = tuple(int(v) for v in np.cumsum(PROJ_SIZES)[:-1])


def rmsnorm(x, g):
    xf = x.astype(jnp.float32)
    y = xf * lax.rsqrt(jnp.mean(xf * xf, axis=-1, keepdims=True) + EPS)
    return y.astype(x.dtype) * g

def grouped_rmsnorm(x, g, groups):
    shp = x.shape
    xf = x.astype(jnp.float32).reshape(shp[:-1] + (groups, shp[-1] // groups))
    y = xf * lax.rsqrt(jnp.mean(xf * xf, axis=-1, keepdims=True) + EPS)
    return y.reshape(shp).astype(x.dtype) * g

def swiglu_2(x, wg, wu, wd):
    return (jax.nn.silu(x @ wg) * (x @ wu)) @ wd

def causal_depthwise_conv(x, w):
    k, c = w.shape
    return lax.conv_general_dilated(
        x, w.reshape(k, 1, c).astype(x.dtype), window_strides=(1,), padding=[(k - 1, 0)],
        dimension_numbers=("NWC", "WIO", "NWC"), feature_group_count=c)

def ssd_chunked(xdt, a, bm, cm):
    b, s, h, p = xdt.shape
    g, n = bm.shape[2], bm.shape[3]
    r = h // g
    nc, L = s // SSM_CHUNK, SSM_CHUNK
    dt_ = xdt.dtype
    X = xdt.reshape(b, nc, L, g, r, p)
    A = a.reshape(b, nc, L, g, r).astype(jnp.float32)
    Bc = bm.reshape(b, nc, L, g, n)
    Cc = cm.reshape(b, nc, L, g, n)
    a_cum = jnp.cumsum(A, axis=2)
    causal = jnp.tril(jnp.ones((L, L), dtype=bool))[None, None, :, :, None, None]
    diff = a_cum[:, :, :, None] - a_cum[:, :, None, :]
    decay = jnp.exp(jnp.where(causal, diff, -jnp.inf)).astype(dt_)
    cb = jnp.einsum("bclgn,bcsgn->bclsg", Cc, Bc)
    y_diag = jnp.einsum("bclsg,bclsgr,bcsgrp->bclgrp", cb, decay, X)
    decay_to_end = jnp.exp(a_cum[:, :, -1:] - a_cum).astype(dt_)
    states = jnp.einsum("bclgn,bclgr,bclgrp->bcgrpn", Bc, decay_to_end, X)
    chunk_decay = jnp.exp(a_cum[:, :, -1]).astype(dt_)

    def step(carry, inp):
        st, dec = inp
        return carry * dec[..., None, None] + st, carry

    init = jnp.zeros((b, g, r, p, n), dtype=states.dtype)
    _, prev = lax.scan(step, init, (jnp.swapaxes(states, 0, 1), jnp.swapaxes(chunk_decay, 0, 1)))
    prev = jnp.swapaxes(prev, 0, 1)
    y_off = jnp.einsum("bclgn,bcgrpn,bclgr->bclgrp", Cc, prev, jnp.exp(a_cum).astype(dt_))
    return (y_diag + y_off).reshape(b, s, h, p)

def hybrid_mixer_2(u, w_in, sc_conv_w, sc_w_out, m_conv_w, m_conv_b, m_dt_bias, m_A_log, m_D,
                 m_norm, m_w_out, w_o):
    b, s, _ = u.shape
    proj = u @ w_in
    sc_b, sc_c, sc_x, m_z, m_xbc, m_dt, gate_a, gate_m = jnp.split(proj, PROJ_SPLITS, axis=-1)
    y_a = (sc_b * causal_depthwise_conv(sc_c * sc_x, sc_conv_w)) @ sc_w_out
    xbc = jax.nn.silu(causal_depthwise_conv(m_xbc, m_conv_w) + m_conv_b)
    xs, bm, cm = jnp.split(xbc, (SSM_INNER, SSM_INNER + SSM_GROUPS * SSM_STATE), axis=-1)
    dt = jax.nn.softplus((m_dt + m_dt_bias).astype(jnp.float32))
    A = -jnp.exp(m_A_log.astype(jnp.float32))
    xh = xs.reshape(b, s, SSM_HEADS, SSM_HEADDIM)
    y = ssd_chunked(xh * dt.astype(xh.dtype)[..., None], A * dt,
                    bm.reshape(b, s, SSM_GROUPS, SSM_STATE), cm.reshape(b, s, SSM_GROUPS, SSM_STATE))
    y = (y + m_D[:, None] * xh).reshape(b, s, SSM_INNER)
    y_m = grouped_rmsnorm(y * jax.nn.silu(m_z), m_norm, SSM_GROUPS) @ m_w_out
    merged = jax.nn.sigmoid(gate_a) * y_a + jax.nn.sigmoid(gate_m) * y_m
    return merged @ w_o

def second_inputs(seed: int = 0) -> dict:
    key = jax.random.key(seed)
    ks = iter(jax.random.split(key, 40))

    def nrm(shape, fan_in):
        return jax.random.normal(next(ks), shape, jnp.float32) * (fan_in ** -0.5)

    def gain(shape):
        return 1.0 + 0.05 * jax.random.normal(next(ks), shape, jnp.float32)

    dt0 = jnp.exp(jax.random.uniform(next(ks), (DEPTH_2, SSM_HEADS), jnp.float32)
                  * (np.log(0.1) - np.log(0.001)) + np.log(0.001))
    return {
        "x": jax.random.normal(next(ks), (BATCH, SEQ, D_MODEL), jnp.float32),
        "p": jax.random.normal(next(ks), (DEPTH_2, BATCH, SEQ, PLE_DIM), jnp.float32),
        "ffn1_norm": gain((DEPTH_2, D_MODEL)),
        "ffn1_wg": nrm((DEPTH_2, D_MODEL, D_FF), D_MODEL),
        "ffn1_wu": nrm((DEPTH_2, D_MODEL, D_FF), D_MODEL),
        "ffn1_wd": nrm((DEPTH_2, D_FF, D_MODEL), D_FF),
        "mix_norm": gain((DEPTH_2, D_MODEL)),
        "w_in": nrm((DEPTH_2, D_MODEL, PROJ_DIM), D_MODEL),
        "sc_conv_w": nrm((DEPTH_2, SC_KERNEL, SC_WIDTH), SC_KERNEL),
        "sc_w_out": nrm((DEPTH_2, SC_WIDTH, D_MODEL), SC_WIDTH),
        "m_conv_w": nrm((DEPTH_2, SSM_CONV, SSM_CONV_DIM), SSM_CONV),
        "m_conv_b": 0.02 * jax.random.normal(next(ks), (DEPTH_2, SSM_CONV_DIM), jnp.float32),
        "m_dt_bias": dt0 + jnp.log(-jnp.expm1(-dt0)),
        "m_A_log": jnp.log(jax.random.uniform(next(ks), (DEPTH_2, SSM_HEADS), jnp.float32, 1.0, 16.0)),
        "m_D": gain((DEPTH_2, SSM_HEADS)),
        "m_norm": gain((DEPTH_2, SSM_INNER)),
        "m_w_out": nrm((DEPTH_2, SSM_INNER, D_MODEL), SSM_INNER),
        "w_o": nrm((DEPTH_2, D_MODEL, D_MODEL), D_MODEL),
        "ffn2_norm": gain((DEPTH_2, D_MODEL)),
        "ffn2_wg": nrm((DEPTH_2, D_MODEL, D_FF), D_MODEL),
        "ffn2_wu": nrm((DEPTH_2, D_MODEL, D_FF), D_MODEL),
        "ffn2_wd": nrm((DEPTH_2, D_FF, D_MODEL), D_FF),
        "ple_norm": gain((DEPTH_2, D_MODEL)),
        "ple_w_gate": nrm((DEPTH_2, D_MODEL, D_MODEL), D_MODEL),
        "ple_w_proj": nrm((DEPTH_2, PLE_DIM, D_MODEL), PLE_DIM),
        "final_norm": gain((D_MODEL,)),
    }

def second_block(x, p, ffn1_norm, ffn1_wg, ffn1_wu, ffn1_wd, mix_norm, w_in, sc_conv_w, sc_w_out,
              m_conv_w, m_conv_b, m_dt_bias, m_A_log, m_D, m_norm, m_w_out, w_o,
              ffn2_norm, ffn2_wg, ffn2_wu, ffn2_wd, ple_norm, ple_w_gate, ple_w_proj, final_norm):
    h = x
    for i in range(DEPTH_2):
        h = h + 0.5 * swiglu_2(rmsnorm(h, ffn1_norm[i]), ffn1_wg[i], ffn1_wu[i], ffn1_wd[i])
        h = h + hybrid_mixer_2(rmsnorm(h, mix_norm[i]), w_in[i], sc_conv_w[i], sc_w_out[i],
                             m_conv_w[i], m_conv_b[i], m_dt_bias[i], m_A_log[i], m_D[i],
                             m_norm[i], m_w_out[i], w_o[i])
        h = h + 0.5 * swiglu_2(rmsnorm(h, ffn2_norm[i]), ffn2_wg[i], ffn2_wu[i], ffn2_wd[i])
        gate = jax.nn.sigmoid(rmsnorm(h, ple_norm[i]) @ ple_w_gate[i])
        h = h + gate * (p[i] @ ple_w_proj[i])
    return rmsnorm(h, final_norm)


def setup_inputs(seed=0):
    out = dict(first_inputs(seed))
    for name, value in second_inputs(seed + 1).items():
        if name != "x":
            out[name + "_2"] = value
    return out


def reference(
    x, mem, ffn1_pre_norm, ffn1_w_gate, ffn1_w_up, ffn1_w_down, ffn1_post_norm, mix_pre_norm,
    w_in, fox_f_bias, gdn_conv_w, gdn_a_log, gdn_dt_bias, gdn_out_norm, w_out, mix_post_norm,
    mem_pre_norm, mem_kv_norm, mem_w_q, mem_w_kv, mem_w_o, mem_post_norm, ffn2_pre_norm,
    ffn2_w_gate, ffn2_w_up, ffn2_w_down, ffn2_post_norm, p_2, ffn1_norm_2, ffn1_wg_2, ffn1_wu_2,
    ffn1_wd_2, mix_norm_2, w_in_2, sc_conv_w_2, sc_w_out_2, m_conv_w_2, m_conv_b_2, m_dt_bias_2,
    m_A_log_2, m_D_2, m_norm_2, m_w_out_2, w_o_2, ffn2_norm_2, ffn2_wg_2, ffn2_wu_2, ffn2_wd_2,
    ple_norm_2, ple_w_gate_2, ple_w_proj_2, final_norm_2,
):
    x = first_block(
        x, mem, ffn1_pre_norm, ffn1_w_gate, ffn1_w_up, ffn1_w_down, ffn1_post_norm,
        mix_pre_norm, w_in, fox_f_bias, gdn_conv_w, gdn_a_log, gdn_dt_bias, gdn_out_norm, w_out,
        mix_post_norm, mem_pre_norm, mem_kv_norm, mem_w_q, mem_w_kv, mem_w_o, mem_post_norm,
        ffn2_pre_norm, ffn2_w_gate, ffn2_w_up, ffn2_w_down, ffn2_post_norm,
    )
    return second_block(
        x, p_2, ffn1_norm_2, ffn1_wg_2, ffn1_wu_2, ffn1_wd_2, mix_norm_2, w_in_2, sc_conv_w_2,
        sc_w_out_2, m_conv_w_2, m_conv_b_2, m_dt_bias_2, m_A_log_2, m_D_2, m_norm_2, m_w_out_2,
        w_o_2, ffn2_norm_2, ffn2_wg_2, ffn2_wu_2, ffn2_wd_2, ple_norm_2, ple_w_gate_2,
        ple_w_proj_2, final_norm_2,
    )


_drawn_inputs = setup_inputs


def setup_inputs(seed=0):
    import zlib

    import numpy as np

    out = dict(_drawn_inputs(seed))
    spreads = {}
    factors = {'ffn1_pre_norm': 2.833,
     'ffn1_post_norm': 3.912,
     'gdn_out_norm': 3.965,
     'mix_post_norm': 3.423,
     'mem_pre_norm': 4.176,
     'mem_kv_norm': 2.818,
     'mem_post_norm': 3.893,
     'ffn2_pre_norm': 5.996,
     'ffn2_post_norm': 24.636,
     'ffn1_norm_2': 3.264,
     'm_conv_b_2': 5.867,
     'm_D_2': 19.426,
     'm_norm_2': 10.627,
     'ffn2_norm_2': 3.911,
     'ple_norm_2': 64.0}
    for name, (base, spread) in spreads.items():
        noise = np.random.default_rng([zlib.crc32(name.encode()), seed]).standard_normal(out[name].shape)
        drawn = base * np.exp(spread * noise) if base else spread * noise
        out[name] = __import__('jax').numpy.asarray(drawn.astype(out[name].dtype))
    for name, factor in factors.items():
        out[name] = (out[name] * factor).astype(out[name].dtype)
    return out
```

```python
from contextlib import ExitStack

import numpy as np
import concourse.bass as bass
import concourse.mybir as mybir

F32 = mybir.dt.float32
F32R = mybir.dt.float32r
ALU = mybir.AluOpType
ACT = mybir.ActivationFunctionType
AX_X = mybir.AxisListType.X
ADD, SUB, MUL, MAX, MIN = ALU.add, ALU.subtract, ALU.mult, ALU.max, ALU.min

P = 128
T = 256
D = 1024
KT = D // P
D_FF = 2816
FT = D_FF // P
EPS = 1e-6
FOX_H, FOX_D = 8, 64
GDN_H, GDN_D, CHUNK = 4, 128, 64
MEM_H, MEM_D = 4, 256
SSM_H, SSM_P, SSM_G, SSM_L = 32, 64, 4, 128
DEPTH_2 = 2
CE = 1024
RAW, SPLIT = 4, 4

CONSTS = ["ident", "tri", "ones", "later", "tri64", "later64", "strict64",
          "merge1", "merge2", "merge4", "merge8", "merge16", "merge32", "neg"]


def constant_matrices():
    s, t = np.arange(P)[:, None], np.arange(P)[None, :]
    same = s // CHUNK == t // CHUNK
    out = {
        "ident": s == t, "tri": s <= t, "ones": s >= 0 * t, "later": s > t,
        "tri64": same & (s <= t), "later64": same & (s > t), "strict64": same & (s < t),
        "neg": (t > s) * -(2.0 ** 100),
    }
    for b in (1, 2, 4, 8, 16, 32):
        out[f"merge{b}"] = (s // (2 * b) == t // (2 * b)) & (s % (2 * b) < b) & (t % (2 * b) >= b)
    return np.ascontiguousarray(np.stack([out[n].astype(np.float32) for n in CONSTS], axis=1))


FIRST_BLOCKS = [("xbc", 4), ("c", 0), ("xbc", 5), ("c", 1), ("xbc", 0), ("x", 0), ("xbc", 1), ("x", 1),
                ("xbc", 2), ("xbc", 3)]

PARAMS = [
    ("ffn1_pre_norm", 8), ("ffn1_post_norm", 8), ("mix_pre_norm", 8), ("mix_post_norm", 8),
    ("mem_pre_norm", 8), ("mem_kv_norm", 8), ("mem_post_norm", 8), ("ffn2_pre_norm", 8),
    ("ffn2_post_norm", 8), ("gdn_out_norm", 1), ("gdn_conv_w", 48), ("fox_f_bias", 8),
    ("gdn_a_log", 4), ("gdn_dt_bias", 4), ("final_norm_2", 8),
]
for _i in range(DEPTH_2):
    PARAMS += [(f"{n}{_i}", c) for n, c in (
        ("ffn1_norm_2", 8), ("mix_norm_2", 8), ("sc_conv_w_2", 24), ("m_conv_w_2", 96),
        ("m_conv_b_2", 24), ("m_norm_2", 16), ("ffn2_norm_2", 8), ("ple_norm_2", 8), ("m_D_2", 16),
        ("m_dt_bias_2", 32), ("m_A_log_2", 32))]
PARAM_AT = {}
for _n, _c in PARAMS:
    PARAM_AT[_n] = (sum(c for _, c in list(PARAMS)[:[n for n, _ in PARAMS].index(_n)]), _c)
N_PARAMS = sum(c for _, c in PARAMS)


class Token:

    def __init__(self, sem, value):
        self.sem, self.value = sem, value


def flat(after):
    for a in after:
        if isinstance(a, Token):
            yield a
        elif a is not None:
            yield from flat(a)


class Queue:

    def __init__(self, sem):
        self.sem, self.count, self.ops, self.seen = sem, 0, [], {}

    def wait(self, *after):
        need = {}
        for t in flat(after):
            if t.value > max(self.seen.get(id(t.sem), 0), need.get(id(t.sem), (None, 0))[1]):
                need[id(t.sem)] = (t.sem, t.value)
        for key, (sem, value) in need.items():
            self.seen[key] = value
            self.ops.append(lambda e, sem=sem, value=value: e.wait_ge(sem, value))

    def run(self, op, after=()):
        self.wait(after)
        self.count += 1
        self.ops.append(lambda e: op(e).then_inc(self.sem, 1))
        return Token(self.sem, self.count)

    def last(self):
        return Token(self.sem, self.count) if self.count else None


class Tensor(Queue):
    def group(self, matmuls, after=()):
        self.wait(after)
        self.count += 1
        n = len(matmuls)
        for i, (out, lhs, rhs, start) in enumerate(matmuls):
            def op(e, out=out, lhs=lhs, rhs=rhs, start=start, i=i):
                mm = e.matmul(out, lhs, rhs, start=start, stop=True, skip_group_check=True)
                if i == n - 1:
                    mm.then_inc(self.sem, 1)
            self.ops.append(op)
        return Token(self.sem, self.count)

    def transposes(self, pairs, ident, after=()):
        self.wait(after)
        self.count += 1
        for i, (out, src) in enumerate(pairs):
            def op(e, out=out, src=src, i=i):
                mm = e.transpose(out, src, ident)
                if i == len(pairs) - 1:
                    mm.then_inc(self.sem, 1)
            self.ops.append(op)
        return Token(self.sem, self.count)


class Vector(Queue):
    def tt(self, out, a, b, op, after=()):
        return self.run(lambda e: e.tensor_tensor(out, a, b, op), after)

    def ts(self, out, a, s1, op0, s2=None, op1=None, after=()):
        if op1 is None:
            return self.run(lambda e: e.tensor_scalar(out, a, s1, None, op0), after)
        return self.run(lambda e: e.tensor_scalar(out, a, s1, s2, op0, op1), after)

    def ts_max(self, out, a, s1, row_max, after=()):
        return self.run(lambda e: e.tensor_scalar(out, a, s1, None, ADD, MAX, accum_out=row_max), after)

    def stt(self, out, a, s, b, op0, op1, after=()):
        return self.run(lambda e: e.scalar_tensor_tensor(
            out=out, in0=a, scalar=s, in1=b, op0=op0, op1=op1), after)

    def copy(self, out, a, after=()):
        return self.run(lambda e: e.tensor_copy(out, a), after)

    def recip(self, out, a, after=()):
        return self.run(lambda e: e.reciprocal(out, a), after)

    def rmax(self, out, a, after=()):
        return self.run(lambda e: e.tensor_reduce(out, a, AX_X, MAX), after)

    def zero(self, out, after=()):
        return self.run(lambda e: e.memset(out, 0.0), after)


class Scalar(Queue):
    def act(self, out, a, func, after=(), **kw):
        return self.run(lambda e: e.activation(out, a, func, **kw), after)

    def copy(self, out, a, after=()):
        return self.run(lambda e: e.copy(out, a), after)


class Loads(Queue):

    def load(self, dst, src, sem, n=1, after=()):
        self.wait(after)
        self.ops.append(lambda e: e.dma_start(dst, src).then_inc(sem, 16))
        return Token(sem, 16 * n)


class Ring:

    def __init__(self, bufs):
        self.idle = [(b, None) for b in bufs]

    def take(self):
        assert self.idle, "no buffer is free at this point of the program"
        return self.idle.pop(0)

    def give(self, buf, readers):
        self.idle.append((buf, readers))


def weave(main, side, every=1, start=0):
    for n, _ in enumerate(main):
        if n >= start and (n - start) % every == 0:
            next(side, None)
    drain(side)


def in_turn(*gens):
    gens = list(gens)
    while gens:
        for g in list(gens):
            if next(g, "end") == "end":
                gens.remove(g)
            else:
                yield


def one_by_one(*gens):
    for g in gens:
        yield from g


def drain(gen):
    for _ in gen:
        pass


class Chunk:

    def __init__(self, w, k0, nk, c0, nc, m0=0, slot=0):
        self.src = w[k0 * P:(k0 + nk) * P, c0:c0 + nc].rearrange("(k p) n -> p k n", p=P)
        self.k0, self.nk, self.nc, self.m0, self.slot = k0, nk, nc, m0, slot


def column_blocks(w, c0, c1):
    kt = w.shape[0] // P
    step = CE // 512
    return [[Chunk(w, k, min(step, kt - k), c, 512) for k in range(0, kt, step)]
            for c in range(c0, c1, 512)]


def halved_block(w):
    kt = w.shape[0] // P
    step = CE // 512
    return [[Chunk(w, k, step, 512 * slot, 512, 0, slot)
             for k1 in (0, kt // 2) for slot in range(2) for k in range(k1, k1 + kt // 2, step)]]


def gate_up_blocks(wg, wu):
    step = CE // 256
    return [[Chunk(w, k, step, c, 256, m) for k in range(0, KT, step) for w, m in ((wg, 0), (wu, 2))]
            for c in range(0, D_FF, 256)]


class Stream:

    def __init__(self, k, chunks):
        self.k, self.chunks = k, chunks
        self.raw = [k.sb(f"w_raw{i}", [P, CE]) for i in range(RAW)]
        self.hi = [k.sb(f"w_hi{i}", [P, CE], F32R) for i in range(SPLIT)]
        self.lo = [k.sb(f"w_lo{i}", [P, CE], F32R) for i in range(SPLIT)]
        self.sem = [k.sem(f"w_landed{i}") for i in range(RAW)]
        self.loaded, self.split, self.used = {}, {}, {}
        self.at = 0
        for i in range(RAW):
            self.load(i)
        for i in range(SPLIT - 1):
            self.prepare(i)

    def load(self, i):
        if i >= len(self.chunks):
            return
        c = self.chunks[i]
        dst = self.raw[i % RAW][:, 0:c.nk * c.nc].rearrange("p (k n) -> p k n", k=c.nk)
        self.loaded[i] = self.k.sp.load(dst, c.src, self.sem[i % RAW], i // RAW + 1,
                                        after=self.split.get(i - RAW))

    def prepare(self, i):
        if i >= len(self.chunks):
            return
        c = self.chunks[i]
        n = c.nk * c.nc
        raw, hi, lo = self.raw[i % RAW], self.hi[i % SPLIT], self.lo[i % SPLIT]
        a = self.k.act.copy(hi[:, 0:n], raw[:, 0:n], after=[self.loaded[i], self.used.get(i - SPLIT)])
        b = self.k.dve.tt(lo[:, 0:n], raw[:, 0:n], hi[:, 0:n].bitcast(F32), SUB, after=a)
        self.split[i] = [a, b]
        self.load(i + RAW)

    def next(self, chunk):
        i = self.at
        assert self.chunks[i] is chunk
        self.at += 1
        self.prepare(i + SPLIT - 1)
        view = lambda x: x[i % SPLIT][:, 0:chunk.nk * chunk.nc].rearrange("p (k n) -> p k n", k=chunk.nk)
        return i, view(self.hi), view(self.lo), self.split[i]


class Scope:
    pass


class Memory:

    def __init__(self, k):
        self.kern, self.scope = k, ExitStack()
        self.k_tok, self.v_tok = [], []
        self.k, self.v, self.f = (k.sb("mem_" + n, s, F32, self.scope)
                                  for n, s in (("k", [P, KT, T]), ("v", [P, 2, D]), ("f", [P, KT, T])))

    def prepare(self, scope):
        kern = self.kern
        self.x = Split(kern, "memn", KT, scope)
        t = kern.gp.load(self.f[:, :, :], kern.ap["mem_t"], kern.sem("mem_landed"))
        tiles = kern.pre_norm(self.f, [t] * KT, "mem_kv_norm", self.x, cols=True)
        tiles(0)
        tiles(4)
        self.taken = [kern.dve.last(), kern.act.last()]

    def ep_k(self, b, acc, done):
        t = self.kern.dve.tt(self.k[:, 4 * b:4 * b + 4, :], acc.rearrange("p (j t) -> p j t", j=4),
                             self.kern.rows(self.x.rms, 4), MUL, after=[done, self.x.rms.tok])
        self.k_tok.append(t)
        return t

    def ep_v(self, b, acc, done):
        t = [self.kern.act.act(self.v[:, i, 512 * b:512 * b + 512], acc[:, 512 * i:512 * i + 512], ACT.Copy,
                               scale=self.x.rms.cols[:, i:i + 1], after=[done, self.x.rms.cols_tok])
             for i in range(2)]
        self.v_tok.append(t)
        return t


class Split:

    def __init__(self, k, name, tiles, stack=None, width=T):
        self.hi = k.sb(name + "_hi", [P, tiles, width], F32R, stack)
        self.lo = k.sb(name + "_lo", [P, tiles, width], F32R, stack)
        self.tok = [None] * tiles


class Kernel:
    def __init__(self, nc, ctx, ap):
        self.nc, self.ctx, self.ap = nc, ctx, ap
        self.pe = Tensor(self.sem("tensor_done"))
        self.dve = Vector(self.sem("vector_done"))
        self.act = Scalar(self.sem("scalar_done"))
        self.sp = Loads(self.sem("sync_done"))
        self.gp = Loads(self.sem("gpsimd_done"))

        acc = [ctx.enter_context(nc.psum_tensor(f"acc{i}", [P, 4 * T], F32)) for i in range(2)]
        small = [ctx.enter_context(nc.psum_tensor(f"small{i}", [P, 512], F32)) for i in range(4)]
        self.acc = Ring([b[:, :] for b in acc])
        self.small = Ring([b[:, :] for b in small])

        self.h = self.sb("h", [P, KT, T])
        self.h_tok = [None] * KT
        self.consts = self.sb("consts_sb", [P, len(CONSTS), P])
        self.params = self.sb("params_sb", [P, N_PARAMS])
        self.sq = self.sb("squares", [P, 4, T])
        self.sq_free = None
        self.rms_rows = Ring([self.sb(f"rms_rows{i}", [P, T])[:, :] for i in range(4)])
        self.rms_cols = Ring([self.sb(f"rms_cols{i}", [P, 2])[:, :] for i in range(4)])
        self.deferred = []
        self.tmp = Ring([self.sb(f"tmp{i}", [P, 4 * T])[:, :] for i in range(2)])
        self.xn = Split(self, "xn", KT)

    def sb(self, name, shape, dtype=F32, stack=None):
        return (stack or self.ctx).enter_context(self.nc.sbuf_tensor(name, shape, dtype))

    def sem(self, name):
        return self.ctx.enter_context(self.nc.semaphore(name))

    def const(self, name):
        return self.consts[:, CONSTS.index(name), :]

    def param(self, name, i=0, n=1):
        at = PARAM_AT[name][0] + i
        return self.params[:, at:at + n]

    def fence(self):
        last = [q.last() for q in (self.pe, self.dve, self.act)]
        for q in (self.dve, self.act, self.gp):
            q.wait(last)

    def defer(self, steps, fn):
        self.deferred.append([steps, fn])

    def step(self):
        for d in list(self.deferred):
            d[0] -= 1
            if d[0] <= 0:
                self.deferred.remove(d)
                d[1]()

    def spread(self, gen):
        def go():
            if next(gen, "end") != "end":
                self.defer(1, go)
        go()

    def linear(self, name, x, epilogue, tokens_out=False):
        for b, block in enumerate(self.linears[name]):
            slots = 1 + max(c.slot for c in block)
            accs = [self.acc.take() for _ in range(slots)]
            for n, chunk in enumerate(block):
                acc, free = accs[chunk.slot]
                i, w_hi, w_lo, w_tok = self.stream.next(chunk)
                for k in range(chunk.nk):
                    kk = chunk.k0 + k
                    mms = []
                    for m in range(2 if tokens_out else chunk.nc // P):
                        if tokens_out:
                            out = acc[:, 512 * m:512 * m + 512]
                            toks = slice(P * m, P * m + P)
                            terms = [(x.hi[:, kk, toks], w_hi[:, k, :]), (x.lo[:, kk, toks], w_hi[:, k, :]),
                                     (x.hi[:, kk, toks], w_lo[:, k, :])]
                            first = kk == 0
                        else:
                            tile = chunk.m0 + m
                            out = acc[:, T * tile:T * tile + T]
                            cols = slice(P * m, P * m + P)
                            terms = [(w_hi[:, k, cols], x.hi[:, kk, :]), (w_hi[:, k, cols], x.lo[:, kk, :]),
                                     (w_lo[:, k, cols], x.hi[:, kk, :])]
                            first = kk == 0 and tile % 2 == 0
                        mms += [(out, lhs, rhs, first and n == 0) for n, (lhs, rhs) in enumerate(terms)]
                    done = self.pe.group(mms, after=[w_tok, x.tok[kk], free])
                    self.stream.used[i] = done
                    self.step()
                    yield
                if all(c.slot != chunk.slot for c in block[n + 1:]):
                    self.acc.give(acc, epilogue(slots * b + chunk.slot, acc, done))

    def narrow(self, x, w, out):
        mms = []
        for t in range(2):
            toks = slice(P * t, P * t + P)
            for k in range(KT):
                for n, (lhs, rhs) in enumerate([(x.hi, w.hi), (x.lo, w.hi), (x.hi, w.lo)]):
                    mms.append((out[t], lhs[:, k, toks], rhs[:, k, :], t == 0 and k == 0 and n == 0))
        return mms

    def split_from(self, src, x, j, n, after):
        hi, lo = x.hi[:, j:j + n, :], x.lo[:, j:j + n, :]
        src = src.rearrange("p (j t) -> p j t", j=n)
        a = self.act.copy(hi, src, after=after)
        b = self.dve.tt(lo, src, hi.bitcast(F32), SUB, after=a)
        for i in range(j, j + n):
            x.tok[i] = b
        return b

    def squares(self, src, after, total=None):
        a = self.act.act(self.sq[:, :, :], src, ACT.Square, after=[after, self.sq_free])
        b = self.dve.tt(self.sq[:, 0:2, :], self.sq[:, 0:2, :], self.sq[:, 2:4, :], ADD, after=a)
        if total is None:
            out, free = self.rms_rows.take()
            t = self.dve.tt(out, self.sq[:, 0, :], self.sq[:, 1, :], ADD, after=[b, free])
        else:
            out = total[0]
            c = self.dve.tt(self.sq[:, 0, :], self.sq[:, 0, :], self.sq[:, 1, :], ADD, after=b)
            t = self.dve.tt(out, out, self.sq[:, 0, :], ADD, after=[c, total[1]])
        self.sq_free = t
        return out, t

    def inverse_rms(self, total, width, cols=False):
        r = Scope()
        r.cols = None
        sums, tok = total
        bank, free = self.small.take()
        mms = [(bank[:, 0:T], self.const("ones"), sums, True)]
        if cols:
            mms += [(bank[:, T + i:T + i + 1], sums[:, P * i:P * i + P], self.const("ones")[:, 0:1], False)
                    for i in range(2)]
        t = self.pe.group(mms, after=[tok, free])
        root = dict(scale=1.0 / width, bias=self.eps[:, 0:1])
        a = self.act.act(sums, bank[:, 0:T], ACT.Sqrt, after=t, **root)
        if cols:
            r.cols, cfree = self.rms_cols.take()
            a = self.act.act(r.cols, bank[:, T:T + 2], ACT.Sqrt, after=[t, cfree], **root)
            r.cols_tok = self.dve.recip(r.cols, r.cols, after=a)
        self.small.give(bank, a)
        r.rows = sums
        r.tok = self.dve.recip(sums, sums, after=a)
        return r

    def release(self, r):
        last = [self.dve.last(), self.act.last()]
        self.rms_rows.give(r.rows, last)
        if r.cols is not None:
            self.rms_cols.give(r.cols, last)

    def rows(self, r, n):
        return r.rows.unsqueeze(1).to_broadcast([P, n, T])

    def pre_norm(self, src, toks, gain, x, cols=False):
        total = []
        readers = []

        def tiles(j):
            if not readers:
                readers.append(self.pe.last())
            for i in range(j, j + 4):
                g = self.param(gain, i)
                a = self.act.act(x.hi[:, i, :], src[:, i, :], ACT.Copy, scale=g, after=[toks[i], readers])
                x.tok[i] = self.dve.stt(x.lo[:, i, :], src[:, i, :], g, x.hi[:, i, :].bitcast(F32), MUL, SUB,
                                        after=a)
            total.append(self.squares(src[:, j:j + 4, :], toks[j:j + 4], total[0] if total else None))
            if len(total) == 2:
                def finish():
                    x.rms = self.inverse_rms(total[1], D, cols)
                self.defer(3, finish)
        return tiles

    def add_normed(self, f, toks, gain, factor, then):
        total = []

        def tiles(j):
            total.append(self.squares(f[:, j:j + 4, :], toks[j:j + 4], total[0] if total else None))

        def finish():
            r = self.inverse_rms(total[1], D)
            for j in range(KT):
                t = self.dve.stt(f[:, j, :], f[:, j, :], self.param(gain, j), r.rows, MUL, MUL,
                                 after=[r.tok, toks[j]])
                self.h_tok[j] = self.dve.stt(self.h[:, j, :], f[:, j, :], factor, self.h[:, j, :], MUL, ADD,
                                             after=[t, self.h_tok[j]])
                if j % 4 == 3:
                    then(j - 3)
            self.release(r)
        return tiles, finish

    def to_buffer(self, f, toks, then=None):
        def epilogue(b, acc, done):
            t = self.dve.copy(f[:, 4 * b:4 * b + 4, :], acc.rearrange("p (j t) -> p j t", j=4), after=done)
            toks[4 * b:4 * b + 4] = [t] * 4
            if then:
                then(4 * b)
            return t
        return epilogue

    def to_residual(self, factor, then):
        def epilogue(b, acc, done):
            h = self.h[:, 4 * b:4 * b + 4, :]
            t = self.dve.stt(h, acc.rearrange("p (j t) -> p j t", j=4), factor, h, MUL, ADD,
                             after=[done, self.h_tok[4 * b:4 * b + 4]])
            self.h_tok[4 * b:4 * b + 4] = [t] * 4
            then(4 * b)
            return t
        return epilogue

    def ffn(self, name, then, post_gain=None):
        with ExitStack() as scope:
            hid = Split(self, name + "_hidden", FT, scope)
            f = self.sb(name + "_f", [P, KT, T], F32, scope) if post_gain else None
            f_tok = [None] * KT

            def hidden(b, acc, done):
                r = self.xn.rms
                tmp, free = self.tmp.take()
                part = lambda x, i: x[:, 512 * i:512 * i + 512].rearrange("p (j t) -> p j t", j=2)
                g = self.dve.tt(part(tmp, 0), part(acc, 0), self.rows(r, 2), MUL, after=[done, free, r.tok])
                u = self.dve.tt(part(tmp, 1), part(acc, 1), self.rows(r, 2), MUL, after=[done, free, r.tok])
                a = self.act.act(tmp[:, 0:512], tmp[:, 0:512], ACT.Silu, after=g)
                m = self.dve.tt(tmp[:, 0:512], tmp[:, 0:512], tmp[:, 512:1024], MUL, after=[a, u])
                self.tmp.give(tmp, self.split_from(tmp[:, 0:512], hid, 2 * b, 2, m))
                return [g, u]

            drain(self.linear(name + "_gate_up", self.xn, hidden))
            self.release(self.xn.rms)
            if post_gain:
                tiles, finish = self.add_normed(f, f_tok, post_gain, 0.5, then)
                drain(self.linear(name + "_down", hid, self.to_buffer(f, f_tok, tiles)))
                finish()
            else:
                drain(self.linear(name + "_down", hid, self.to_residual(0.5, then)))
            self.fence()

    def conv(self, taps, weight, tile0, n_tiles, src, dst, after, bias=None):
        rows = [self.act.act(dst[:, i, :], src[:, i, 0:T], ACT.Identity,
                             scale=self.param(weight, tile0 + i),
                             bias=self.param(bias, tile0 + i) if bias else 0.0, after=after)
                for i in range(4)]
        for k in range(1, taps):
            yield
            for i in range(4):
                rows[i] = self.dve.stt(dst[:, i, :], src[:, i, k:k + T],
                                       self.param(weight, n_tiles * k + tile0 + i), dst[:, i, :], MUL, ADD,
                                       after=[rows[i], after])
        return rows

    def softplus(self, x, scratch, after):
        a = self.dve.ts(scratch, x, -1.0, MUL, after=after)
        a = self.dve.tt(scratch, scratch, x, MIN, after=a)
        a = self.act.act(scratch, scratch, ACT.Exp, after=a)
        a = self.act.act(scratch, scratch, ACT.Ln, bias=self.one[:, 0:1], after=a)
        return self.dve.stt(x, x, 0.0, scratch, MAX, ADD, after=a)

    def fox_attention(self, q, k, v, ls, tok, mixed, fox, mem):
        pe, dve, act = self.pe, self.dve, self.act
        ident = self.const("ident")
        fq, neg_ls, stat = fox.F, fox.neg_ls, fox.stat
        bufs = mem.f[:, 0:6, :].rearrange("p j t -> p (j t)").rearrange("p (h a n) -> p h a n", h=2, a=2)

        bank, free = self.small.take()
        t = pe.group([(bank[:, 0:8], self.const("tri"), ls[:, 0, :], True),
                      (bank[:, 8:16], self.const("ones"), ls[:, 0, :], False),
                      (bank[:, 8:16], self.const("tri"), ls[:, 1, :], False)], after=[tok, free])
        fq_tok = dve.copy(fq[:, :, :], bank[:, 0:16].rearrange("p (a b) -> p a b", a=2), after=t)
        self.small.give(bank, fq_tok)
        yield
        neg_free, p_free = None, mem.taken
        parts = [(slice(0, 128), 0), (slice(128, 384), 1)]
        tri2 = self.consts[:, 1:3, :].rearrange("p a t -> p (a t)")
        for j in range(FOX_H // 2):
            ready = []
            for half in range(2):
                h = 2 * j + half
                rows = slice(FOX_D * half, FOX_D * half + FOX_D)
                neg = neg_ls[:, 2 * half:2 * half + 2, :]
                t = dve.ts(neg, ls[:, :, h:h + 1].to_broadcast([P, 2, P]), -1.0, MUL, after=[tok, neg_free])
                bank, free = self.small.take()
                lo, hi = bank[:, 0:128], bank[:, 128:384]
                s = pe.group([
                    (lo, q[rows, j, 0:P], k[rows, j, 0:P], True),
                    (lo, neg[:, 0, :], self.const("tri"), False),
                    (lo, ident, self.const("neg"), False),
                    (hi, q[rows, j, P:T], k[rows, j, :], True),
                    (hi, neg[:, 0, :], tri2, False),
                    (hi[:, P:T], neg[:, 1, :], self.const("tri"), False),
                    (hi[:, P:T], ident, self.const("neg"), False)], after=[tok, t, free])
                p = bufs[:, half, 0, :]
                m = [dve.ts_max(p[:, c], bank[:, c], fq[:, i, h:h + 1], stat[:, h, i:i + 1],
                                after=[s, p_free, fq_tok]) for c, i in parts]
                self.small.give(bank, m)
                n = dve.ts(stat[:, h, 2:4], stat[:, h, 0:2], -1.0, MUL, after=m)
                e = [act.act(p[:, c], p[:, c], ACT.Exp, bias=stat[:, h, 2 + i:3 + i],
                             accum_out=stat[:, h, 4 + i:5 + i], after=n) for c, i in parts]
                ready.append(e)
                if half == 0:
                    yield
            neg_free = s
            d = []
            for half in range(2):
                h, p = 2 * j + half, bufs[:, half, 0, :]
                r = dve.recip(stat[:, h, 4:6], stat[:, h, 4:6], after=ready[half])
                d.append([dve.ts(p[:, c], p[:, c], stat[:, h, 4 + i:5 + i], MUL, after=r) for c, i in parts])
            yield
            turned = []
            for half in range(2):
                p, pT = bufs[:, half, 0, :], bufs[:, half, 1, :]
                bank, free = self.small.take()
                t = pe.transposes([(bank[:, P * i:P * i + P], p[:, P * i:P * i + P]) for i in range(3)], ident,
                                  after=[d[half], free])
                turned.append(act.copy(pT, bank[:, 0:384], after=t))
                self.small.give(bank, turned[-1])
            yield
            bank, free = self.small.take()
            mms = []
            for half in range(2):
                h, pT = 2 * j + half, bufs[:, half, 1, :]
                o = bank[FOX_D * half:FOX_D * half + FOX_D, 0:T]
                vh = slice(FOX_D * h, FOX_D * h + FOX_D)
                mms += [(o, v[:, 0, vh], pT[:, 0:T], True), (o[:, P:T], v[:, 1, vh], pT[:, T:384], False)]
            p_free = t = pe.group(mms, after=[turned, free, tok])
            self.small.give(bank, self.split_from(bank[:, 0:T], mixed, j, 1, t))
            yield

    def gdn_prepare(self, g, c, c_tok, small_tok):
        pe, dve, act = self.pe, self.dve, self.act
        ident, ones = self.const("ident"), self.const("ones")
        H4 = GDN_H
        beta, a = g.raw[:, :, 0:4], g.raw[:, :, 4:8]
        t_beta = act.act(beta, beta, ACT.Sigmoid, after=small_tok)
        t = dve.tt(a, a, self.param("gdn_dt_bias", 0, 4).unsqueeze(1).to_broadcast([P, 2, 4]), ADD,
                   after=small_tok)
        t = self.softplus(a, g.scratch[:, :, 0:4], t)
        ea = act.act(g.scratch[:, 0, 4:8], self.param("gdn_a_log", 0, 4), ACT.Exp, after=small_tok)
        t_a = dve.stt(a, a, -1.0, g.scratch[:, 0:1, 4:8].to_broadcast([P, 2, 4]), MUL, MUL, after=[t, ea])
        yield
        bank, free = self.small.take()
        mms = [(bank[:, 8 * i + 4 * m:8 * i + 4 * m + 4], self.const(n), a[:, i, :], i + m == 0)
               for i in range(2) for m, n in enumerate(("tri64", "later64"))]
        t = pe.group(mms, after=[t_a, free])
        v = bank[:, 0:16].rearrange("p (i m) -> p i m", i=2)
        t_neg = dve.ts(g.neg_cum[:, :, :], v[:, :, 0:4], -1.0, MUL, after=t)
        t1 = act.act(g.e_cum_tail[:, :, :], v, ACT.Exp, after=t_neg)
        self.small.give(bank, t1)
        t_bg = dve.tt(g.beta_ecum[:, :, :], g.e_cum_tail[:, :, 0:4], beta, MUL, after=[t1, t_beta])
        t_ab = dve.copy(g.rep[:, 0:8, :].rearrange("p (i h) t -> p i h t", i=2),
                        a.unsqueeze(3).to_broadcast([P, 2, 4, P]), after=t_a)
        t_bb = dve.copy(g.rep[:, 8:16, :].rearrange("p (i h) t -> p i h t", i=2),
                        beta.unsqueeze(3).to_broadcast([P, 2, 4, P]), after=t_beta)
        yield
        norm_tok = [None] * 8
        for j in range(0, 8, 2):
            tmp, free = self.tmp.take()
            s = act.act(tmp[:, 0:512], c[:, j:j + 2, :].rearrange("p a t -> p (a t)"), ACT.Square,
                        after=[c_tok[j // 4], free])
            bank, bfree = self.small.take()
            t = pe.group([(bank, ones, tmp[:, 0:512], True)], after=[s, bfree])
            a1 = act.act(tmp[:, 512:1024], bank, ACT.Sqrt, bias=self.eps[:, 0:1], after=t)
            self.small.give(bank, a1)
            r = dve.recip(tmp[:, 512:1024], tmp[:, 512:1024], after=a1)
            dst = (g.qn if j < 4 else g.kn)[:, j % 4:j % 4 + 2, :]
            t = dve.stt(dst, c[:, j:j + 2, :], GDN_D ** -0.5 if j < 4 else 1.0,
                        tmp[:, 512:1024].rearrange("p (a t) -> p a t", a=2), MUL, MUL, after=r)
            self.tmp.give(tmp, t)
            norm_tok[j] = norm_tok[j + 1] = t
            yield
        for i in range(2):
            toks = slice(P * i, P * i + P)
            bank, free = self.small.take()
            t = pe.transposes([(bank[:, P * h:P * h + P], c[:, 8 + h, toks]) for h in range(H4)], ident,
                              after=[c_tok[2], free])
            out = [dve.ts(g.vb[:, i, h, :], bank[:, P * h:P * h + P], beta[:, i, h:h + 1], MUL,
                          after=[t, t_beta]) for h in range(H4)]
            self.small.give(bank, out)
            g.tok_vb[i] = out
            bank, free = self.small.take()
            t = pe.transposes([(bank[:, P * h:P * h + P], g.kn[:, h, toks]) for h in range(H4)], ident,
                              after=[norm_tok[4:8], free])
            out = [dve.ts(dst[:, i, h, :], bank[:, P * h:P * h + P], s[:, i, o + h:o + h + 1], MUL,
                          after=[t, t_bg])
                   for dst, s, o in ((g.kbg, g.beta_ecum, 0), (g.ktail, g.e_cum_tail, 4)) for h in range(H4)]
            self.small.give(bank, out)
            g.tok_k[i] = out
            yield
            bank, free = self.small.take()
            t = pe.group([(bank[:, P * h:P * h + P], g.rep[:, 4 * i + h, :], self.const("tri64"), True)
                          for h in range(H4)], after=[t_ab, free])
            e1 = act.act(g.e_rows[:, i, :, :].rearrange("p h t -> p (h t)"), bank, ACT.Exp, after=t)
            dec, dfree = self.tmp.take()
            e2 = [dve.ts(dec[:, P * h:P * h + P], bank[:, P * h:P * h + P], g.neg_cum[:, i, h:h + 1], ADD,
                         0.0, MIN, after=[t_neg, dfree, e1]) for h in range(H4)]
            self.small.give(bank, e2)
            e2 = act.act(dec[:, 0:512], dec[:, 0:512], ACT.Exp, after=e2)
            g.tok_rows[i] = e1
            g.tok_qd[i] = dve.tt(g.qd[:, :, toks], g.qn[:, :, toks], g.e_rows[:, i, :, :], MUL,
                                 after=[e1, norm_tok[0:4]])
            dv = dec[:, 0:512].rearrange("p (h t) -> p h t", h=H4)
            rep = lambda n: self.const(n).unsqueeze(1).to_broadcast([P, H4, P])
            t = dve.tt(dv, dv, rep("tri64"), MUL, after=e2)
            qk, free = self.small.take()
            m = pe.group([(qk[:, P * h:P * h + P], g.kn[:, h, toks], g.qn[:, h, toks], True)
                          for h in range(H4)], after=[norm_tok, free])
            t1 = dve.tt(g.attn[:, i, :, :].rearrange("p h t -> p (h t)"), qk, dec[:, 0:512], MUL, after=[t, m])
            self.small.give(qk, t1)
            g.tok_attn[i] = t1
            yield
            bb, free = self.small.take()
            m = pe.group([(bb[:, P * h:P * h + P], g.rep[:, 8 + 4 * i + h, :], ident, True)
                          for h in range(H4)], after=[t_bb, free])
            t = dve.tt(dv, dv, rep("strict64"), MUL, after=t1)
            t = dve.tt(dec[:, 0:512], dec[:, 0:512], bb, MUL, after=[t, m])
            self.small.give(bb, t)
            kk, free = self.small.take()
            m = pe.group([(kk[:, P * h:P * h + P], g.kn[:, h, toks], g.kn[:, h, toks], True)
                          for h in range(H4)], after=free)
            g.tok_L[i] = dve.tt(g.LT[:, i, :, :].rearrange("p h t -> p (h t)"), kk, dec[:, 0:512], MUL,
                                after=[t, m])
            self.small.give(kk, g.tok_L[i])
            self.tmp.give(dec, g.tok_L[i])
            yield

    def gdn_invert(self, g):
        pe, dve, act = self.pe, self.dve, self.act
        ident = self.const("ident")
        H4 = GDN_H
        rep = lambda n: self.const(n).unsqueeze(1).to_broadcast([P, H4, P])
        flat2 = lambda x, i: x[:, i, :, :].rearrange("p h t -> p (h t)")
        blk = lambda b, h: b[:, P * h:P * h + P]
        tok_x, tok_xt, n_tok, y_free, n_free = [None] * 2, [None] * 2, [None] * 2, [None] * 2, [None] * 2
        for i in range(2):
            n_tok[i] = dve.tt(g.NT[:, i, :, :], g.LT[:, i, :, :], rep("merge1"), MUL, after=g.tok_L[i])
            tok_xt[i] = dve.tt(g.XT[:, i, :, :], rep("ident"), g.NT[:, i, :, :], SUB, after=n_tok[i])
        for i in range(2):
            bank, free = self.small.take()
            t = pe.transposes([(blk(bank, h), g.XT[:, i, h, :]) for h in range(H4)], ident,
                              after=[tok_xt[i], free])
            tok_x[i] = act.copy(flat2(g.X, i), bank, after=t)
            n_free[i] = tok_xt[i]
            self.small.give(bank, tok_x[i])
        yield
        for b in (2, 4, 8, 16, 32):
            ys = []
            for i in range(2):
                n_tok[i] = dve.tt(g.NT[:, i, :, :], g.LT[:, i, :, :], rep(f"merge{b}"), MUL, after=n_free[i])
            for i in range(2):
                bank, free = self.small.take()
                t = pe.group([(blk(bank, h), g.NT[:, i, h, :], g.X[:, i, h, :], True) for h in range(H4)],
                             after=[n_tok[i], tok_x[i], free])
                n_free[i] = t
                y = act.copy(flat2(g.Y, i), bank, after=[t, y_free[i]])
                self.small.give(bank, y)
                ys.append(y)
            yield
            for i in range(2):
                y = ys[i]
                banks = []
                for part in (0, 1) if b < 32 else (1,):
                    bank, free = self.small.take()
                    mms = [(blk(bank, h), g.XT[:, i, h, :], g.Y[:, i, h, :], True) if part == 0 else
                           (blk(bank, h), g.Y[:, i, h, :], g.XT[:, i, h, :], True) for h in range(H4)]
                    t = pe.group(mms, after=[y, free, tok_xt[i]])
                    banks.append((part, bank, t))
                y_free[i] = t
                for part, bank, t1 in banks:
                    x = g.X if part == 0 else g.XT
                    r = dve.tt(flat2(x, i), flat2(x, i), bank, SUB, after=[t1, t])
                    self.small.give(bank, r)
                    if part == 0:
                        tok_x[i] = r
                    else:
                        tok_xt[i] = r
            yield
        for i in range(2):
            bank, free = self.small.take()
            t = pe.group([(blk(bank, h), g.XT[:, i, h, :], g.vb[:, i, h, :], True) for h in range(H4)],
                         after=[tok_xt[i], g.tok_vb[i], free])
            g.tok_u[i] = act.copy(flat2(g.u, i), bank, after=t)
            self.small.give(bank, g.tok_u[i])
            bank, free = self.small.take()
            t = pe.group([(blk(bank, h), g.kbg[:, i, h, :], g.XT[:, i, h, :], True) for h in range(H4)],
                         after=[tok_xt[i], g.tok_k[i], free])
            g.tok_w[i] = dve.copy(flat2(g.wT, i), bank, after=t)
            self.small.give(bank, g.tok_w[i])
            yield

    def gdn_scan(self, g, gz, gz_tok, mixed):
        pe, dve, act = self.pe, self.dve, self.act
        H4 = GDN_H
        blk = lambda b, h: b[:, P * h:P * h + P]
        s_tok, vn_free, s_free = None, None, None
        for c in range(T // CHUNK):
            i, lo = c // 2, CHUNK * (c % 2)
            rows = slice(lo, lo + CHUNK)
            cols = slice(P * i + lo, P * i + lo + CHUNK)
            if c:
                bank, free = self.small.take()
                t = pe.group([(blk(bank, h), g.wT[:, i, h, :], g.S[:, h, :], True) for h in range(H4)],
                             after=[s_tok, g.tok_w[i], free])
                vn = dve.tt(g.vn[rows, :, :].rearrange("p h e -> p (h e)"),
                            g.u[rows, i, :, :].rearrange("p h e -> p (h e)"), bank[rows, :], SUB,
                            after=[t, g.tok_u[i], vn_free])
                self.small.give(bank, vn)
            else:
                vn = dve.copy(g.vn[rows, :, :], g.u[rows, i, :, :], after=g.tok_u[i])
            yield
            if lo == 0:
                o_bank, o_free = self.small.take()
            mms = []
            for h in range(H4):
                o = o_bank[:, P * h + lo:P * h + lo + CHUNK]
                if c:
                    mms.append((o, g.S[:, h, :], g.qd[:, h, cols], True))
                mms.append((o, g.vn[rows, h, :], g.attn[rows, i, h, rows], c == 0))
            t_o = pe.group(mms, after=[vn, g.tok_qd[i], g.tok_attn[i], o_free])
            vn_free = t_o
            if c < T // CHUNK - 1:
                bank, free = self.small.take()
                t = pe.group([(blk(bank, h), g.ktail[rows, i, h, :], g.vn[rows, h, :], True)
                              for h in range(H4)], after=[free, g.tok_k[i]])
                vn_free = t
                if c:
                    s_tok = [dve.stt(g.S[:, h, :], g.S[:, h, :], g.e_rows[:, i, h, lo + 63:lo + 64],
                                     blk(bank, h), MUL, ADD, after=[t, g.tok_rows[i]]) for h in range(H4)]
                else:
                    s_tok = dve.copy(g.S[:, :, :].rearrange("p h e -> p (h e)"), bank, after=t)
                self.small.give(bank, s_tok)
            if lo:
                o3 = o_bank.rearrange("p (h t) -> p h t", h=H4)
                tmp, free = self.tmp.take()
                sq, rs = tmp[:, 0:512], tmp[:, 512:1024]
                a = act.act(sq, o_bank, ACT.Square, after=[t_o, free])
                bank, bfree = self.small.take()
                t = pe.group([(bank, self.const("ones"), sq, True)], after=[a, bfree])
                a = act.act(rs, bank, ACT.Sqrt, scale=1.0 / GDN_D, bias=self.eps[:, 0:1], after=t)
                self.small.give(bank, a)
                r = dve.recip(rs, rs, after=a)
                t = dve.stt(sq, o_bank, self.param("gdn_out_norm"), rs, MUL, MUL, after=[r])
                self.small.give(o_bank, t)
                z = gz[:, :, P * i:P * i + P]
                t = dve.tt(sq.rearrange("p (h t) -> p h t", h=H4), sq.rearrange("p (h t) -> p h t", h=H4), z,
                           MUL, after=[t, gz_tok])
                x_hi, x_lo = (x[:, 4:8, P * i:P * i + P] for x in (mixed.hi, mixed.lo))
                s3 = sq.rearrange("p (h t) -> p h t", h=H4)
                a = act.copy(x_hi, s3, after=t)
                t = dve.tt(x_lo, s3, x_hi.bitcast(F32), SUB, after=a)
                self.tmp.give(tmp, t)
                mixed.tok[4:8] = [[mixed.tok[4 + n], t] for n in range(4)]
            yield

    def hybrid_mixer(self, mem):
        pe, dve, act = self.pe, self.dve, self.act
        r = self.xn
        with ExitStack() as scope:
            sb = lambda n, s, st=scope: self.sb("m1_" + n, s, F32, st)
            mixed = Split(self, "mixed", KT, scope)
            q, k = sb("fq", [P, 4, T]), sb("fk", [P, 4, T])
            v = sb("fv", [P, 2, 512])
            ls, ls_tmp = sb("ls", [P, 2, 8]), sb("ls_tmp", [P, 2, 8])
            fox, g = Scope(), Scope()
            fox.F, fox.neg_ls = sb("fox_F", [P, 2, FOX_H]), sb("fox_neg_ls", [P, 4, P])
            fox.stat = sb("fox_stat", [P, FOX_H, 6])
            g.raw, g.scratch = sb("g_raw", [P, 2, 8]), sb("g_scratch", [P, 2, 8])
            g.neg_cum, g.e_cum_tail = sb("g_neg_cum", [P, 2, 4]), sb("g_e_cum_tail", [P, 2, 8])
            g.beta_ecum = sb("g_beta_ecum", [P, 2, 4])
            g.S, g.vn, g.qd, gz = sb("g_S", [P, 4, P]), sb("g_vn", [P, 4, P]), sb("g_qd", [P, 4, T]), sb("gz", [P, 4, T])
            g.ktail, g.e_rows, g.attn, g.u, g.wT = (
                sb("g_" + n, [P, 2, 4, P]) for n in ("ktail", "e_rows", "attn", "u", "wT"))
            early = scope.enter_context(ExitStack())
            c = sb("conv_out", [P, 12, T], early)
            cin = sb("conv_in", [P, 4, T + 3], early)
            g.rep = mem.k[:, :, :].rearrange("p j t -> p (j t)").rearrange("p (j t) -> p j t", j=16)
            g.qn, g.kn = mem.f[:, 0:4, :], mem.f[:, 4:8, :]
            g.vb, g.kbg = (mem.v[:, i, :].rearrange("p (i h t) -> p i h t", i=2, h=4) for i in range(2))
            g.LT = g.wT
            as4 = lambda x: x.rearrange("p a t -> p (a t)").rearrange("p (i h t) -> p i h t", i=2, h=4)
            g.X, g.XT, g.Y = as4(c[:, 0:4, :]), as4(c[:, 4:8, :]), as4(c[:, 8:12, :])
            g.NT = as4(g.rep[:, 0:8, :])
            g.tok_vb, g.tok_k, g.tok_rows, g.tok_qd, g.tok_attn, g.tok_L, g.tok_u, g.tok_w = (
                [None, None] for _ in range(8))

            pad = dve.zero(cin[:, :, 0:3])
            tok, c_tok, gz_tok = {}, [None] * 3, []
            state = {"cin": pad}
            four = lambda acc: acc.rearrange("p (j t) -> p j t", j=4)

            def ep_conv(b, acc, done):
                a = dve.tt(cin[:, :, 3:3 + T], four(acc), self.rows(r.rms, 4), MUL,
                           after=[done, state["cin"], r.rms.tok])
                dst = c[:, 4 * b:4 * b + 4, :]

                def steps():
                    state["cin"] = t = yield from self.conv(
                        4, "gdn_conv_w", 4 * b, 12, cin, dst, [a, pad])
                    c_tok[b] = act.act(dst, dst, ACT.Silu, after=t)
                self.spread(steps())
                return a

            def ep_q(b, acc, done):
                tok["q"] = dve.stt(q[:, :, :], four(acc), FOX_D ** -0.5, self.rows(r.rms, 4), MUL, MUL, after=done)
                return tok["q"]

            def ep_k(b, acc, done):
                tok["k"] = dve.tt(k[:, :, :], four(acc), self.rows(r.rms, 4), MUL, after=done)
                return tok["k"]

            def ep_v(b, acc, done):
                tok["v"] = [act.act(v[:, i, :], acc[:, 512 * i:512 * i + 512], ACT.Copy,
                                    scale=r.rms.cols[:, i:i + 1], after=[done, r.rms.cols_tok])
                            for i in range(2)]
                return tok["v"]

            def ep_z(b, acc, done):
                a = dve.tt(gz[:, :, :], four(acc), self.rows(r.rms, 4), MUL, after=done)
                gz_tok.append(act.act(gz[:, :, :], gz[:, :, :], ACT.Silu, after=a))
                return a

            drain(self.linear("gdn_qkv", self.xn, ep_conv))
            bank, free = self.small.take()
            b3 = bank[:, 0:32].rearrange("p (i m) -> p i m", i=2)
            t = pe.group(self.narrow(self.xn, self.w_gates, [b3[:, 0, :], b3[:, 1, :]]),
                         after=[free, self.w_gates_tok, self.xn.tok])
            t = [dve.stt(out[:, i, :], b3[:, i, 8 * n:8 * n + 8], r.rms.cols[:, i:i + 1],
                         self.param("fox_f_bias", 0, 8), MUL, ADD, after=t) if n == 0 else
                 dve.ts(out[:, i, :], b3[:, i, 8 * n:8 * n + 8], r.rms.cols[:, i:i + 1], MUL, after=t)
                 for n, out in enumerate((ls, g.raw)) for i in range(2)]
            small_tok = t
            self.small.give(bank, t)
            t = dve.ts(ls[:, :, :], ls[:, :, :], -1.0, MUL, after=t)
            t = self.softplus(ls[:, :, :], ls_tmp[:, :, :], t)
            tok["ls"] = dve.ts(ls[:, :, :], ls[:, :, :], -1.0, MUL, after=t)

            weave(one_by_one(self.linear("fox_q", self.xn, ep_q), self.linear("fox_k", self.xn, ep_k),
                             self.linear("fox_v", self.xn, ep_v, tokens_out=True),
                             self.linear("gdn_z", self.xn, ep_z)),
                  one_by_one(self.gdn_prepare(g, c, c_tok, small_tok), self.gdn_invert(g)), start=2)
            self.release(self.xn.rms)
            early.close()
            self.fence()
            late = scope.enter_context(ExitStack())
            mem.prepare(late)

            attention = self.fox_attention(q, k, v, ls, [tok[n] for n in ("q", "k", "v", "ls")], mixed, fox, mem)
            weave(one_by_one(self.linear("mem_k", mem.x, mem.ep_k),
                             self.linear("mem_v0", mem.x, mem.ep_v, tokens_out=True)),
                  in_turn(self.gdn_scan(g, gz, gz_tok, mixed), attention))

            f, f_tok = mem.f, [None] * KT
            pre = self.pre_norm(self.h, self.h_tok, "mem_pre_norm", self.xn)
            tiles, finish = self.add_normed(f, f_tok, "mix_post_norm", 1.0, pre)
            drain(self.linear("w_out", mixed, self.to_buffer(f, f_tok, tiles)))
            self.defer(2, finish)
            drain(self.linear("mem_v1", mem.x, lambda b, acc, done: mem.ep_v(1, acc, done), tokens_out=True))

    def memory_attention(self, mem, then):
        pe, dve, act = self.pe, self.dve, self.act
        ident = self.const("ident")
        with ExitStack() as scope:
            sb = lambda n, s: self.sb("mem_" + n, s, F32, scope)
            k, v, q = mem.k, mem.v, sb("q", [P, KT, T])
            o = Split(self, "mem_o", KT, scope)
            f, f_tok = mem.f, [None] * KT
            bufs = Ring([sb(f"p{i}", [P, 2, 512]) for i in range(2)])
            stat = sb("stat", [P, MEM_H, 6])
            q_tok = [None, None]

            def ep_q(b, acc, done):
                q_tok[b] = dve.stt(q[:, 4 * b:4 * b + 4, :], acc.rearrange("p (j t) -> p j t", j=4),
                                   MEM_D ** -0.5, self.rows(self.xn.rms, 4), MUL, MUL,
                                   after=[done, self.xn.rms.tok])
                return q_tok[b]

            def head(h):
                bank, free = self.small.take()
                s = pe.group([(bank[:, T * i:T * i + T], q[:, 2 * h + d, P * i:P * i + P], k[:, 2 * h + d, :],
                               d == 0) for i in range(2) for d in range(2)],
                             after=[q_tok[h // 2], mem.k_tok, free])
                buf, free = bufs.take()
                p, pT = buf[:, 0, :], buf[:, 1, :]
                m = dve.rmax(stat[:, h, 0:2], bank.rearrange("p (i m) -> p i m", i=2), after=s)
                n = dve.ts(stat[:, h, 2:4], stat[:, h, 0:2], -1.0, MUL, after=m)
                e = [act.act(p[:, T * i:T * i + T], bank[:, T * i:T * i + T], ACT.Exp,
                             bias=stat[:, h, 2 + i:3 + i], accum_out=stat[:, h, 4 + i:5 + i],
                             after=[n, free]) for i in range(2)]
                self.small.give(bank, e)
                r = dve.recip(stat[:, h, 4:6], stat[:, h, 4:6], after=e)
                d = [dve.ts(p[:, T * i:T * i + T], p[:, T * i:T * i + T], stat[:, h, 4 + i:5 + i], MUL,
                            after=r) for i in range(2)]
                yield
                bank, free = self.small.take()
                t = pe.transposes([(bank[:, T * mt + P * i:T * mt + P * i + P],
                                    p[:, T * i + P * mt:T * i + P * mt + P])
                                   for mt in range(2) for i in range(2)], ident, after=[d, free])
                c = act.copy(pT, bank, after=t)
                self.small.give(bank, c)
                yield
                bank, free = self.small.take()
                t = pe.group([(bank[:, T * d:T * d + T],
                               v[:, mt, MEM_D * h + P * d:MEM_D * h + P * d + P],
                               pT[:, T * mt:T * mt + T], mt == 0) for d in range(2) for mt in range(2)],
                             after=[c, free, mem.v_tok])
                bufs.give(buf, t)
                self.small.give(bank, self.split_from(bank, o, 2 * h, 2, t))
                yield

            weave(self.linear("mem_q", self.xn, ep_q), in_turn(head(0), head(1)), start=KT + 2)
            self.release(self.xn.rms)
            tiles, finish = self.add_normed(f, f_tok, "mem_post_norm", 1.0, then)
            weave(self.linear("mem_o", o, self.to_buffer(f, f_tok, tiles)), in_turn(head(2), head(3)))
            finish()
        mem.scope.close()
        self.fence()

    def ssd(self, L, s, scope):
        pe, dve, act = self.pe, self.dve, self.act
        ident = self.const("ident")
        blk = lambda b, h: b[:, P * h:P * h + P]
        HG = SSM_H // SSM_G
        dt, a = s.dt, s.a
        bank, free = self.small.take()
        t = pe.group([(bank[:, 0:32], self.const("tri"), a[:, 0, :], True),
                      (bank[:, 32:64], self.const("tri"), a[:, 1, :], True),
                      (bank[:, 64:96], self.const("later"), a[:, 0, :], True)], after=[s.a_tok, free])
        t_neg = dve.ts(s.neg_cum[:, :, :].rearrange("p i h -> p (i h)"), bank[:, 0:64], -1.0, MUL, after=t)
        t_end = act.act(s.to_end[:, :], bank[:, 64:96], ACT.Exp, after=t_neg)
        self.small.give(bank, t_end)
        yield
        bank, free = self.small.take()
        t = pe.transposes([(blk(bank, g), s.bc[:, g, 0:P]) for g in range(SSM_G)], ident,
                          after=[s.bc_tok, free])
        b_tok = act.copy(s.b_rows[:, :, :].rearrange("p g n -> p (g n)"), bank, after=t)
        self.small.give(bank, b_tok)
        yield
        x_tok = {}
        for i in range(2):
            for g in range(SSM_G):
                bank, free = self.small.take()
                t = pe.transposes([(blk(bank, j), s.x[:, 4 * g + j, P * i:P * i + P]) for j in range(4)], ident,
                                  after=[s.x_tok[g], free])
                x_tok[i, g] = dve.tt(
                    s.xdt[:, i, 512 * g:512 * g + 512].rearrange("p (h d) -> p h d", h=HG),
                    bank.rearrange("p (h d) -> p h d", h=HG),
                    dt[:, i, HG * g:HG * g + HG].unsqueeze(2).to_broadcast([P, HG, SSM_P]), MUL,
                    after=[t, s.dt_tok])
                self.small.give(bank, x_tok[i, g])
                yield
        free = Scope()
        free.rep, free.state, free.xe, free.cb = [None, None], [None, None], None, [None, None]
        xe_tok, st_tok, cb_tok, r_tok = {}, {}, {}, {}
        stages = [(g, i, half) for g in range(SSM_G) for i in range(2) for half in range(2)]

        def scale_x(g):
            xe_tok[g] = dve.tt(s.xe[:, :].rearrange("p (h d) -> p h d", h=HG),
                               s.xdt[:, 0, 512 * g:512 * g + 512].rearrange("p (h d) -> p h d", h=HG),
                               s.to_end[:, HG * g:HG * g + HG].unsqueeze(2).to_broadcast([P, HG, SSM_P]), MUL,
                               after=[t_end, x_tok[0, g], free.xe])

        def state_of(g):
            bank, bfree = self.small.take()
            free.xe = t = pe.group([(bank, s.b_rows[:, g, :], s.xe[:, :], True)], after=[xe_tok[g], b_tok, bfree])
            st_tok[g] = act.copy(s.state[g % 2], bank, after=[t, free.state[g % 2]])
            self.small.give(bank, st_tok[g])

        def repeat(n):
            if n < len(stages):
                g, i, half = stages[n]
                h0 = HG * g + 4 * half
                r_tok[n] = act.copy(s.rep[:, n % 2, :, :],
                                    a[:, i, h0:h0 + 4].unsqueeze(2).to_broadcast([P, 4, P]),
                                    after=[s.a_tok, free.rep[n % 2]])

        def products(g, i):
            toks = slice(P * i, P * i + P)
            bank, bfree = self.small.take()
            t = pe.group([(bank[:, 0:P], s.bc[:, g, toks], s.bc[:, 4 + g, toks], True)], after=bfree)
            cb_tok[g, i] = dve.tt(s.cb[i], bank[:, 0:P], self.const("tri"), MUL, after=[t, free.cb[i]])
            self.small.give(bank, cb_tok[g, i])

        repeat(0)
        repeat(1)
        scale_x(0)
        yield
        products(0, 0)
        yield
        late = None
        for n, (g, i, half) in enumerate(stages):
            st = Scope()
            st.n, st.g, st.i, st.half, st.h0 = n, g, i, half, HG * g + 4 * half
            self.ssd_decay(s, st, free, [r_tok[n], t_neg])
            repeat(n + 2)
            if i == 0 and half == 1:
                state_of(g)
            yield
            self.ssd_mask(s, st, free, cb_tok[g, i])
            if late:
                self.ssd_output(L, s, late, free, [x_tok[late.i, late.g], st_tok[late.g] if late.i else None])
            late = st
            if half == 1 and n + 1 < len(stages):
                products(*stages[n + 1][0:2])
            if half == 1 and i == 1 and g + 1 < SSM_G:
                scale_x(g + 1)
            yield
        self.ssd_output(L, s, late, free, [x_tok[late.i, late.g], st_tok[late.g]])
        yield

    def ssd_decay(self, s, st, free, ready):
        pe, dve, act = self.pe, self.dve, self.act
        blk = lambda b, h: b[:, P * h:P * h + P]
        bank, bfree = self.small.take()
        free.rep[st.n % 2] = t = pe.group([(blk(bank, n), s.rep[:, st.n % 2, n, :], self.const("tri"), True)
                                 for n in range(4)], after=[ready, bfree])
        st.m, mfree = s.m.take()
        d_tok = [dve.ts(blk(st.m, n), blk(bank, n), s.neg_cum[:, st.i, st.h0 + n:st.h0 + n + 1], ADD, 0.0, MIN,
                        after=[t, mfree, ready]) for n in range(4)]
        st.e_tok = act.act(st.m[:, :], st.m[:, :], ACT.Exp, after=d_tok)
        st.ep = st.ep_tok = None
        if st.i == 1:
            st.ep, epfree = s.e_pair.take()
            b4 = bank.rearrange("p (n t) -> p n t", n=4)
            st.ep_tok = [act.act(st.ep[64 * r:64 * r + 64, :, :], b4[64 * r:64 * r + 64, r:4:2, :],
                                 ACT.Exp, after=[d_tok, epfree]) for r in range(2)]
        self.small.give(bank, [d_tok, st.ep_tok])

    def ssd_mask(self, s, st, free, cb_tok):
        m3 = st.m[:, :].rearrange("p (n t) -> p n t", n=4)
        free.cb[st.i] = st.m_tok = self.dve.tt(m3, m3, s.cb[st.i].unsqueeze(1).to_broadcast([P, 4, P]), MUL,
                                               after=[st.e_tok, cb_tok])

    def ssd_output(self, L, s, st, free, ready):
        pe, dve = self.pe, self.dve
        g, i, half, m, ep = st.g, st.i, st.half, st.m, st.ep
        toks = slice(P * i, P * i + P)
        j = st.h0 // 2
        yb, bfree = self.small.take()
        mms = []
        for n in range(4):
            h = st.h0 + n
            o = yb[64 * (n % 2):64 * (n % 2) + 64, P * (n // 2):P * (n // 2) + P]
            mms.append((o, s.xdt[:, i, 64 * h:64 * h + 64], m[:, P * n:P * n + P], True))
        if i == 1:
            mms += [(yb[:, T + P * n:T + P * n + P],
                     s.state[g % 2][:, P * (2 * half + n):P * (2 * half + n) + P],
                     s.bc[:, 4 + g, toks], True) for n in range(2)]
        t = pe.group(mms, after=[st.m_tok, bfree, ready])
        s.m.give(m, t)
        free.state[g % 2] = t
        if i == 1:
            pair = lambda x: x.rearrange("p (n t) -> p n t", n=2)
            t = dve.tt(ep[:, :, :], ep[:, :, :], pair(yb[:, T:2 * T]), MUL, after=[t, st.ep_tok])
            t = dve.tt(ep[:, :, :], ep[:, :, :], pair(yb[:, 0:T]), ADD, after=t)
            self.small.give(yb, t)
            src = [ep[:, n, :] for n in range(2)]
        else:
            src = [yb[:, P * n:P * n + P] for n in range(2)]
        y = [dve.stt(s.x[:, j + n, toks], s.x[:, j + n, toks], self.param(f"m_D_2{L}", j + n), src[n],
                     MUL, ADD, after=t) for n in range(2)]
        if i == 1:
            s.e_pair.give(ep, y)
        else:
            self.small.give(yb, y)
        for n in range(2):
            s.y_tok[j + n].append(y[n])

    def hybrid_mixer_2(self, L, then):
        pe, dve, act = self.pe, self.dve, self.act
        with ExitStack() as outer:
            osb = lambda n, s: self.sb(f"m2{L}_" + n, s, F32, outer)
            s = Scope()
            s.x, s.bc = osb("x", [P, 16, T]), osb("bc", [P, 8, T])
            cx, sgm = osb("cx", [P, 8, T + 2]), osb("gate_m", [P, 8, T])
            ya = cx[:, :, 0:T]
            s.x_tok, s.y_tok = [None] * 4, [[] for _ in range(16)]
            inner = outer.enter_context(ExitStack())
            sb = lambda n, s_, d=F32: self.sb(f"m2{L}_" + n, s_, d, inner)
            cin = sb("conv_in", [P, 4, T + 3])
            s.dt, s.a, s.neg_cum = (sb(n, [P, 2, SSM_H]) for n in ("dt", "a", "neg_cum"))
            s.dt_tmp, s.to_end, s.e_a = sb("dt_tmp", [P, 2, SSM_H]), sb("to_end", [P, SSM_H]), sb("e_a", [P, SSM_H])
            s.b_rows, s.xdt = sb("b_rows", [P, 4, P]), sb("xdt", [P, 2, 2048])
            s.xe = sb("xe", [P, 512])
            s.state = [sb(f"state{i}", [P, 512])[:, :] for i in range(2)]
            s.cb = [sb(f"cb{i}", [P, P])[:, :] for i in range(2)]
            s.rep = sb("rep", [P, 2, 4, P])
            s.m = Ring([sb(f"decay{i}", [P, 512]) for i in range(2)])
            s.e_pair = Ring([sb(f"e_pair{i}", [P, 2, P]) for i in range(2)])
            yain = Split(self, f"m2{L}_sc_in", KT, inner)
            xn = self.xn
            four = lambda acc: acc.rearrange("p (j t) -> p j t", j=4)

            pad = [dve.zero(cin[:, :, 0:3]), dve.zero(cx[:, :, 0:2])]
            ea = act.act(s.e_a[:, :], self.param(f"m_A_log_2{L}", 0, 32), ACT.Exp)
            state = {"cin": pad}
            cx_tok = [None, None]

            def ep_xbc(b, acc, done):
                a = dve.tt(cin[:, :, 3:3 + T], four(acc), self.rows(xn.rms, 4), MUL,
                           after=[done, state["cin"], xn.rms.tok])
                dst = s.x[:, 4 * b:4 * b + 4, :] if b < 4 else s.bc[:, 4 * b - 16:4 * b - 12, :]

                def steps():
                    state["cin"] = t = yield from self.conv(
                        4, f"m_conv_w_2{L}", 4 * b, 24, cin, dst, [a, pad], bias=f"m_conv_b_2{L}")
                    r = act.act(dst, dst, ACT.Silu, after=t)
                    if b < 4:
                        s.x_tok[b] = r
                    else:
                        s.bc_tok[b - 4] = r
                self.spread(steps())
                return a

            def ep_first(n, acc, done):
                kind, b = FIRST_BLOCKS[n]
                if kind == "xbc":
                    return ep_xbc(b, acc, done)
                view = cx[:, 4 * b:4 * b + 4, 2:2 + T]
                if kind == "c":
                    cx_tok[b] = t = dve.tt(view, four(acc), self.rows(xn.rms, 4), MUL,
                                           after=[done, pad, xn.rms.tok])
                else:
                    t = dve.tt(view, view, self.rows(xn.rms, 4), MUL, after=cx_tok[b])
                    cx_tok[b] = t = dve.tt(view, view, four(acc), MUL, after=[done, t])
                return t

            s.bc_tok = [None, None]
            first = self.linear(f"first{L}", xn, ep_first)
            for _ in range(KT + 1):
                next(first)
            bank, free = self.small.take()
            b3 = bank[:, 0:64].rearrange("p (i m) -> p i m", i=2)
            w = self.w_dt[L]
            t = pe.group(self.narrow(xn, w, [b3[:, 0, :], b3[:, 1, :]]),
                         after=[free, self.w_dt_tok[L], xn.tok])
            rep2 = lambda x: x.unsqueeze(1).to_broadcast([P, 2, SSM_H])
            t = [dve.stt(s.dt[:, i, :], b3[:, i, :], xn.rms.cols[:, i:i + 1],
                         self.param(f"m_dt_bias_2{L}", 0, 32), MUL, ADD, after=[t, xn.rms.cols_tok])
                 for i in range(2)]
            self.small.give(bank, t)
            s.dt_tok = self.softplus(s.dt[:, :, :], s.dt_tmp[:, :, :], t)
            s.a_tok = dve.stt(s.a[:, :, :], s.dt[:, :, :], -1.0, rep2(s.e_a[:, :]), MUL, MUL,
                              after=[s.dt_tok, ea])
            drain(first)

            ya_tok, sgm_tok = [None, None], [None, None]

            short = [None, None]

            def short_conv():
                for n in range(2):
                    tmp, free = self.tmp.take()
                    t = yield from self.conv(3, f"sc_conv_w_2{L}", 4 * n, 8,
                                                      cx[:, 4 * n:4 * n + 4, :], four(tmp),
                                                      [cx_tok[n], free, pad])
                    cx_tok[n] = t
                    yield
                    short[n] = tmp, dve.tt(four(tmp), four(tmp), self.rows(xn.rms, 4), MUL, after=t)
                    yield

            def ep_sc_b(n, acc, done):
                tmp, tok = short[n]
                t = dve.tt(four(tmp), four(tmp), four(acc), MUL, after=[tok, done])
                self.tmp.give(tmp, self.split_from(tmp, yain, 4 * n, 4, t))
                return t

            def gate(out, toks, readers):
                def epilogue(b, acc, done):
                    v = out[:, 4 * b:4 * b + 4, :]
                    t = dve.tt(v, four(acc), self.rows(xn.rms, 4), MUL, after=[done, readers])
                    toks[b] = act.act(v, v, ACT.Sigmoid, after=t)
                    return t
                return epilogue

            def ep_ya(b, acc, done):
                v = ya[:, 4 * b:4 * b + 4, :]
                ya_tok[b] = dve.tt(v, v, four(acc), MUL, after=[done, ya_tok[b]])
                return ya_tok[b]

            weave(one_by_one(self.linear(f"gate_m{L}", xn, gate(sgm, sgm_tok, None)),
                             self.linear(f"sc_b{L}", xn, ep_sc_b),
                             self.linear(f"gate_a{L}", xn, gate(ya, ya_tok, cx_tok)),
                             self.linear(f"sc_out{L}", yain, ep_ya)),
                  in_turn(short_conv(), self.ssd(L, s, inner)))
            inner.close()
            reuse = [pe.last(), dve.last(), act.last()]
            yn = Split(self, f"m2{L}_yn", 16, outer)
            busy = []

            def ep_z(b, acc, done):
                y = s.x[:, 4 * b:4 * b + 4, :]
                tmp, free = self.tmp.take()
                a = dve.tt(four(tmp), four(acc), self.rows(xn.rms, 4), MUL, after=[done, free])
                t = act.act(tmp, tmp, ACT.Silu, after=a)
                t = dve.tt(y, y, four(tmp), MUL, after=[t, s.y_tok[4 * b:4 * b + 4]])
                self.tmp.give(tmp, t)
                total = self.squares(y, t)

                def finish():
                    r = self.inverse_rms(total, 512)
                    for j in range(4 * b, 4 * b + 4, 2):
                        tmp, free = self.tmp.take()
                        for i in range(2):
                            t = dve.stt(tmp[:, T * i:T * i + T], s.x[:, j + i, :],
                                        self.param(f"m_norm_2{L}", j + i), r.rows, MUL, MUL, after=[r.tok, free])
                        self.tmp.give(tmp, self.split_from(tmp[:, 0:2 * T], yn, j, 2, [t, reuse]))
                    self.release(r)
                self.defer(4, finish)
                return a

            drain(self.linear(f"z{L}", xn, ep_z))
            self.release(xn.rms)
            x_free = pe.last()

            def ep_merge(b, acc, done):
                v, u = sgm[:, 4 * b:4 * b + 4, :], ya[:, 4 * b:4 * b + 4, :]
                t0 = t = dve.tt(v, v, four(acc), MUL, after=[done, sgm_tok[b]])
                t = dve.tt(v, v, u, ADD, after=[t, ya_tok[b]])
                self.split_from(v.rearrange("p j t -> p (j t)"), xn, 4 * b, 4, [t, x_free])
                return t0

            drain(self.linear(f"m_out{L}", yn, ep_merge))
            done_tiles = []
            drain(self.linear(f"w_o{L}", xn, self.to_residual(1.0, done_tiles.append)))
            for j in done_tiles:
                then(j)
            self.fence()

    def ple(self, L, then):
        pe, dve, act = self.pe, self.dve, self.act
        with ExitStack() as scope:
            p_in = self.sb(f"ple{L}_p", [P, 2, T], F32, scope)
            px = Split(self, f"ple{L}_px", 2, scope)
            proj = self.sb(f"ple{L}_proj", [P, KT, T], F32, scope)
            gate = self.sb(f"ple{L}_gate", [P, KT, T], F32, scope)
            t = self.gp.load(p_in[:, :, :], self.ap["p_t"][L], self.sem(f"p_landed{L}"))
            self.split_from(p_in[:, :, :].rearrange("p a t -> p (a t)"), px, 0, 2, t)
            proj_tok = [None] * KT
            xn = self.xn

            def ep(b, acc, done):
                sl = slice(4 * b, 4 * b + 4)
                a = dve.tt(gate[:, sl, :], acc.rearrange("p (j t) -> p j t", j=4), self.rows(xn.rms, 4), MUL,
                           after=[done, xn.rms.tok])
                t = act.act(gate[:, sl, :], gate[:, sl, :], ACT.Sigmoid, after=a)
                t = dve.tt(gate[:, sl, :], gate[:, sl, :], proj[:, sl, :], MUL, after=[t, proj_tok[sl]])
                t = dve.tt(self.h[:, sl, :], self.h[:, sl, :], gate[:, sl, :], ADD, after=[t, self.h_tok[sl]])
                self.h_tok[sl] = [t] * 4
                return a

            drain(self.linear(f"ple_proj{L}", px, self.to_buffer(proj, proj_tok)))
            drain(self.linear(f"ple_gate{L}", xn, ep))
            then(0)
            then(4)
            self.release(xn.rms)
            self.fence()

    def program(self):
        A = self.ap
        W1, pe, dve, act = A["w_in"][0], self.pe, self.dve, self.act
        L = {}
        L["f1_gate_up"] = gate_up_blocks(A["ffn1_w_gate"][0], A["ffn1_w_up"][0])
        L["f1_down"] = column_blocks(A["ffn1_w_down"][0], 0, D)
        L["gdn_qkv"] = column_blocks(W1, 1544, 3080)
        L["fox_q"] = column_blocks(W1, 0, 512)
        L["fox_k"] = column_blocks(W1, 512, 1024)
        L["fox_v"] = column_blocks(W1, 1024, 1536)
        L["gdn_z"] = column_blocks(W1, 3080, 3592)
        L["mem_k"] = column_blocks(A["mem_w_kv"][0], 0, D)
        L["mem_v0"] = column_blocks(A["mem_w_kv"][0], D, D + 512)
        L["w_out"] = halved_block(A["w_out"][0])
        L["mem_v1"] = column_blocks(A["mem_w_kv"][0], D + 512, 2 * D)
        L["mem_q"] = column_blocks(A["mem_w_q"][0], 0, D)
        L["mem_o"] = halved_block(A["mem_w_o"][0])
        L["f2_gate_up"] = gate_up_blocks(A["ffn2_w_gate"][0], A["ffn2_w_up"][0])
        L["f2_down"] = column_blocks(A["ffn2_w_down"][0], 0, D)
        for i in range(DEPTH_2):
            w = A["w_in_2"][i]
            L[f"g1{i}_gate_up"] = gate_up_blocks(A["ffn1_wg_2"][i], A["ffn1_wu_2"][i])
            L[f"g1{i}_down"] = column_blocks(A["ffn1_wd_2"][i], 0, D)
            at = {"xbc": 5120, "c": 1024, "x": 2048}
            L[f"first{i}"] = [column_blocks(w, at[n] + 512 * b, at[n] + 512 * b + 512)[0]
                              for n, b in FIRST_BLOCKS]
            L[f"gate_m{i}"] = column_blocks(w, 9248, 10272)
            L[f"sc_b{i}"] = column_blocks(w, 0, 1024)
            L[f"gate_a{i}"] = column_blocks(w, 8224, 9248)
            L[f"sc_out{i}"] = column_blocks(A["sc_w_out_2"][i], 0, D)
            L[f"z{i}"] = column_blocks(w, 3072, 5120)
            L[f"m_out{i}"] = column_blocks(A["m_w_out_2"][i], 0, D)
            L[f"w_o{i}"] = halved_block(A["w_o_2"][i])
            L[f"g2{i}_gate_up"] = gate_up_blocks(A["ffn2_wg_2"][i], A["ffn2_wu_2"][i])
            L[f"g2{i}_down"] = column_blocks(A["ffn2_wd_2"][i], 0, D)
            L[f"ple_proj{i}"] = column_blocks(A["ple_w_proj_2"][i], 0, D)
            L[f"ple_gate{i}"] = column_blocks(A["ple_w_gate_2"][i], 0, D)
        self.linears = L

        x_tok = self.gp.load(self.h[:, :, :], A["x_t"], self.sem("x_landed"))
        self.h_tok = [x_tok] * KT
        params_tok = self.gp.load(self.params[:, :], A["params"], self.sem("params_landed"))
        consts_tok = self.gp.load(self.consts[:, :, :], A["consts"], self.sem("consts_landed"))
        for q in (pe, dve, act):
            q.wait(params_tok, consts_tok)
        self.eps, self.one = self.sb("eps", [P, 1]), self.sb("one", [P, 1])
        t0 = dve.run(lambda e: e.memset(self.eps[:, :], EPS))
        t1 = dve.run(lambda e: e.memset(self.one[:, :], 1.0))
        act.wait(t0, t1)

        self.stream = Stream(self, [c for blocks in L.values() for b in blocks for c in b])
        splits = {n: Split(self, n, KT, width=w)
                  for n, w in (("w_gates", 16), ("w_dt0", SSM_H), ("w_dt1", SSM_H))}
        loading = ExitStack()

        def narrow_weights(name, parts, n):
            raw = self.sb(name + "_raw", [P, KT, n], F32, loading)
            w = splits[name]
            at, toks = 0, []
            for part in parts:
                m = part.shape[1]
                toks.append(self.gp.load(raw[:, :, at:at + m], part.rearrange("(k p) n -> p k n", p=P),
                                         self.sem(f"{name}_landed{at}")))
                at += m
            a = act.copy(w.hi[:, :, :], raw[:, :, :], after=toks)
            return w, dve.tt(w.lo[:, :, :], raw[:, :, :], w.hi[:, :, :].bitcast(F32), SUB, after=a)

        self.w_gates, self.w_gates_tok = narrow_weights("w_gates", [W1[:, 1536:1544], W1[:, 3592:3600]], 16)
        self.w_dt, self.w_dt_tok = [], []
        for i in range(DEPTH_2):
            w, t = narrow_weights(f"w_dt{i}", [A["w_in_2"][i][:, 8192:8224]], SSM_H)
            self.w_dt.append(w)
            self.w_dt_tok.append(t)

        loading.close()

        def pre(gain, cols=False):
            return self.pre_norm(self.h, self.h_tok, gain, self.xn, cols)

        start = pre("ffn1_pre_norm")
        start(0)
        start(4)
        self.ffn("f1", pre("mix_pre_norm", cols=True), "ffn1_post_norm")
        mem = Memory(self)
        self.hybrid_mixer(mem)
        self.memory_attention(mem, pre("ffn2_pre_norm"))
        self.ffn("f2", pre("ffn1_norm_20"), "ffn2_post_norm")
        final = []
        for i in range(DEPTH_2):
            self.ffn(f"g1{i}", pre(f"mix_norm_2{i}", cols=True))
            self.hybrid_mixer_2(i, pre(f"ffn2_norm_2{i}"))
            self.ffn(f"g2{i}", pre(f"ple_norm_2{i}"))
            self.ple(i, pre("ffn1_norm_21") if i == 0 else lambda j: final.append(
                self.squares(self.h[:, j:j + 4, :], self.h_tok[j:j + 4], final[0] if final else None)))

        r = self.inverse_rms(final[1], D)
        done = [dve.stt(self.h[:, j, :], self.h[:, j, :], self.param("final_norm_2", j), r.rows,
                        MUL, MUL, after=[r.tok, self.h_tok[j]]) for j in range(KT)]
        stored = self.gp.load(A["out"], self.h[:, :, :], self.sem("out_stored"), after=done)
        self.gp.wait(stored)


def build(nc, ap):
    with ExitStack() as ctx:
        k = Kernel(nc, ctx, ap)
        k.program()
        block = ctx.enter_context(nc.Block())
        for queue, place in ((k.sp, block.sync), (k.gp, block.gpsimd), (k.pe, block.tensor),
                             (k.dve, block.vector), (k.act, block.scalar)):
            def body(e, queue=queue):
                for op in queue.ops:
                    op(e)
            place(body)


WEIGHTS = ["ffn1_w_gate", "ffn1_w_up", "ffn1_w_down", "w_in", "w_out", "mem_w_q", "mem_w_kv", "mem_w_o",
           "ffn2_w_gate", "ffn2_w_up", "ffn2_w_down", "ffn1_wg_2", "ffn1_wu_2", "ffn1_wd_2", "w_in_2",
           "sc_w_out_2", "m_w_out_2", "w_o_2", "ffn2_wg_2", "ffn2_wu_2", "ffn2_wd_2", "ple_w_gate_2",
           "ple_w_proj_2"]


def kernel(**inputs):
    import concourse.bacc as bacc
    from concourse.bass_utils import run_bass_kernel_spmd

    x = {n: np.asarray(a) for n, a in inputs.items()}

    def feature_major(a):
        return np.ascontiguousarray(a.T.reshape(-1, P, a.shape[0]).transpose(1, 0, 2))

    def columns(a):
        return a.reshape(-1, P).T

    rows = ("fox_f_bias", "gdn_a_log", "gdn_dt_bias", "m_dt_bias_2", "m_A_log_2")
    cols = []
    for name, n in PARAMS:
        base, layer = (name[:-1], int(name[-1])) if name not in x else (name, 0)
        a = x[base] if name == "final_norm_2" else x[base][layer]
        if base in rows:
            a = np.broadcast_to(a[None, :], (P, n))
        elif base == "m_D_2":
            a = columns(np.repeat(a, SSM_P))
        else:
            a = columns(a)
        assert a.shape == (P, n), name
        cols.append(a)
    arrays = {n: np.ascontiguousarray(x[n]) for n in WEIGHTS}
    arrays["params"] = np.ascontiguousarray(np.concatenate(cols, axis=1))
    arrays["consts"] = constant_matrices()
    arrays["x_t"] = feature_major(x["x"][0])
    arrays["mem_t"] = feature_major(x["mem"][0])
    arrays["p_t"] = np.stack([feature_major(x["p_2"][i, 0]) for i in range(DEPTH_2)])

    nc = bacc.Bacc("TRN2", target_bir_lowering=False, num_devices=1)
    ap = {n: nc.dram_tensor(n + "_dram", a.shape, F32, kind="ExternalInput").ap() for n, a in arrays.items()}
    ap["out"] = nc.dram_tensor("out_dram", (P, KT, T), F32, kind="ExternalOutput").ap()
    build(nc, ap)
    r = run_bass_kernel_spmd(nc, [{n + "_dram": a for n, a in arrays.items()}], core_ids=[0])
    out = r.results[0]["out_dram"]
    return np.ascontiguousarray(out.transpose(1, 0, 2).reshape(D, T).T)[None]
```

```python
from contextlib import ExitStack

import numpy as np
import concourse.bass as bass
import concourse.mybir as mybir

F32 = mybir.dt.float32
F32R = mybir.dt.float32r
ALU = mybir.AluOpType
ACT = mybir.ActivationFunctionType
AX_X = mybir.AxisListType.X
ADD, SUB, MUL, MAX, MIN = ALU.add, ALU.subtract, ALU.mult, ALU.max, ALU.min

P = 128
T = 256
D = 1024
KT = D // P
D_FF = 2816
FT = D_FF // P
EPS = 1e-6
FOX_H, FOX_D = 8, 64
GDN_H, GDN_D, CHUNK = 4, 128, 64
MEM_H, MEM_D = 4, 256
SSM_H, SSM_P, SSM_G, SSM_L = 32, 64, 4, 128
DEPTH_2 = 2
CE = 1024
FENCE_DELAY = 7
EPILOGUE_DELAY = 4
NORM_PAUSE = 5
RMS_DELAY = 8
RAW, SPLIT = 4, 4

CONSTS = ["ident", "tri", "ones", "later", "tri64", "later64", "strict64",
          "merge1", "merge2", "merge4", "merge8", "merge16", "merge32", "neg"]


def constant_matrices():
    s, t = np.arange(P)[:, None], np.arange(P)[None, :]
    same = s // CHUNK == t // CHUNK
    out = {
        "ident": s == t, "tri": s <= t, "ones": s >= 0 * t, "later": s > t,
        "tri64": same & (s <= t), "later64": same & (s > t), "strict64": same & (s < t),
        "neg": (t > s) * -(2.0 ** 100),
    }
    for b in (1, 2, 4, 8, 16, 32):
        out[f"merge{b}"] = (s // (2 * b) == t // (2 * b)) & (s % (2 * b) < b) & (t % (2 * b) >= b)
    return np.ascontiguousarray(np.stack([out[n].astype(np.float32) for n in CONSTS], axis=1))


FIRST_BLOCKS = [("xbc", 4), ("c", 0), ("xbc", 5), ("c", 1), ("xbc", 0), ("x", 0), ("xbc", 1), ("x", 1),
                ("xbc", 2), ("xbc", 3)]

SCAN_AHEAD = (44, 46, 54, 58, 70, 74)

PARAMS = [
    ("ffn1_pre_norm", 8), ("ffn1_post_norm", 8), ("mix_pre_norm", 8), ("mix_post_norm", 8),
    ("mem_pre_norm", 8), ("mem_kv_norm", 8), ("mem_post_norm", 8), ("ffn2_pre_norm", 8),
    ("ffn2_post_norm", 8), ("gdn_out_norm", 1), ("gdn_conv_w", 48), ("fox_f_bias", 8),
    ("gdn_a_log", 4), ("gdn_dt_bias", 4), ("final_norm_2", 8),
]
for _i in range(DEPTH_2):
    PARAMS += [(f"{n}{_i}", c) for n, c in (
        ("ffn1_norm_2", 8), ("mix_norm_2", 8), ("sc_conv_w_2", 24), ("m_conv_w_2", 96),
        ("m_conv_b_2", 24), ("m_norm_2", 16), ("ffn2_norm_2", 8), ("ple_norm_2", 8), ("m_D_2", 16),
        ("m_dt_bias_2", 32), ("m_A_log_2", 32))]
PARAM_AT = {}
for _n, _c in PARAMS:
    PARAM_AT[_n] = (sum(c for _, c in list(PARAMS)[:[n for n, _ in PARAMS].index(_n)]), _c)
N_PARAMS = sum(c for _, c in PARAMS)


class Token:

    def __init__(self, sem, value):
        self.sem, self.value = sem, value


def flat(after):
    for a in after:
        if isinstance(a, Token):
            yield a
        elif a is not None:
            yield from flat(a)


class Queue:

    def __init__(self, sem):
        self.sem, self.count, self.ops, self.seen = sem, 0, [], {}

    def wait(self, *after):
        need = {}
        for t in flat(after):
            if t.value > max(self.seen.get(id(t.sem), 0), need.get(id(t.sem), (None, 0))[1]):
                need[id(t.sem)] = (t.sem, t.value)
        for key, (sem, value) in need.items():
            self.seen[key] = value
            self.ops.append(lambda e, sem=sem, value=value: e.wait_ge(sem, value))

    def run(self, op, after=()):
        self.wait(after)
        self.count += 1
        self.ops.append(lambda e: op(e).then_inc(self.sem, 1))
        return Token(self.sem, self.count)

    def last(self):
        return Token(self.sem, self.count) if self.count else None


class Tensor(Queue):
    def group(self, matmuls, after=()):
        self.wait(after)
        self.count += 1
        n = len(matmuls)
        for i, (out, lhs, rhs, start) in enumerate(matmuls):
            def op(e, out=out, lhs=lhs, rhs=rhs, start=start, i=i):
                mm = e.matmul(out, lhs, rhs, start=start, stop=True, skip_group_check=True)
                if i == n - 1:
                    mm.then_inc(self.sem, 1)
            self.ops.append(op)
        return Token(self.sem, self.count)

    def transposes(self, pairs, ident, after=()):
        self.wait(after)
        self.count += 1
        for i, (out, src) in enumerate(pairs):
            def op(e, out=out, src=src, i=i):
                mm = e.transpose(out, src, ident)
                if i == len(pairs) - 1:
                    mm.then_inc(self.sem, 1)
            self.ops.append(op)
        return Token(self.sem, self.count)


class Vector(Queue):
    def tt(self, out, a, b, op, after=()):
        return self.run(lambda e: e.tensor_tensor(out, a, b, op), after)

    def ts(self, out, a, s1, op0, s2=None, op1=None, after=()):
        if op1 is None:
            return self.run(lambda e: e.tensor_scalar(out, a, s1, None, op0), after)
        return self.run(lambda e: e.tensor_scalar(out, a, s1, s2, op0, op1), after)

    def ts_max(self, out, a, s1, row_max, after=()):
        return self.run(lambda e: e.tensor_scalar(out, a, s1, None, ADD, MAX, accum_out=row_max), after)

    def stt(self, out, a, s, b, op0, op1, after=()):
        return self.run(lambda e: e.scalar_tensor_tensor(
            out=out, in0=a, scalar=s, in1=b, op0=op0, op1=op1), after)

    def copy(self, out, a, after=()):
        return self.run(lambda e: e.tensor_copy(out, a), after)

    def recip(self, out, a, after=()):
        return self.run(lambda e: e.reciprocal(out, a), after)

    def rmax(self, out, a, after=()):
        return self.run(lambda e: e.tensor_reduce(out, a, AX_X, MAX), after)

    def zero(self, out, after=()):
        return self.run(lambda e: e.memset(out, 0.0), after)


class Scalar(Queue):
    def act(self, out, a, func, after=(), **kw):
        return self.run(lambda e: e.activation(out, a, func, **kw), after)

    def copy(self, out, a, after=()):
        return self.run(lambda e: e.copy(out, a), after)


class Loads(Queue):

    def load(self, dst, src, sem, n=1, after=()):
        self.wait(after)
        self.ops.append(lambda e: e.dma_start(dst, src).then_inc(sem, 16))
        return Token(sem, 16 * n)


class Ring:

    def __init__(self, bufs):
        self.idle = [(b, None) for b in bufs]

    def take(self):
        assert self.idle, "no buffer is free at this point of the program"
        return self.idle.pop(0)

    def give(self, buf, readers):
        self.idle.append((buf, readers))


def weave(main, side, every=1, start=0):
    for n, _ in enumerate(main):
        if n >= start and (n - start) % every == 0:
            next(side, None)
    drain(side)


def in_turn(*gens):
    gens = list(gens)
    while gens:
        for g in list(gens):
            if next(g, "end") == "end":
                gens.remove(g)
            else:
                yield


def one_by_one(*gens):
    for g in gens:
        yield from g


def pause(steps):
    for _ in range(steps):
        yield


def apart(gen, steps):
    for _ in gen:
        yield from pause(steps + 1)


def until(ready):
    while not ready():
        yield


def drain(gen):
    for _ in gen:
        pass


class Chunk:

    def __init__(self, w, k0, nk, c0, nc, m0=0, slot=0):
        self.src = w[k0 * P:(k0 + nk) * P, c0:c0 + nc].rearrange("(k p) n -> p k n", p=P)
        self.k0, self.nk, self.nc, self.m0, self.slot = k0, nk, nc, m0, slot


def column_blocks(w, c0, c1):
    kt = w.shape[0] // P
    step = CE // 512
    return [[Chunk(w, k, min(step, kt - k), c, 512) for k in range(0, kt, step)]
            for c in range(c0, c1, 512)]


def halved_block(w):
    kt = w.shape[0] // P
    step = CE // 512
    return [[Chunk(w, k, step, 512 * slot, 512, 0, slot)
             for k1 in (0, kt // 2) for slot in range(2) for k in range(k1, k1 + kt // 2, step)]]


def gate_up_blocks(wg, wu):
    step = CE // 256
    return [[Chunk(w, k, step, c, 256, m) for k in range(0, KT, step) for w, m in ((wg, 0), (wu, 2))]
            for c in range(0, D_FF, 256)]


class Stream:

    def __init__(self, k, chunks):
        self.k, self.chunks = k, chunks
        self.raw = [k.sb(f"w_raw{i}", [P, CE]) for i in range(RAW)]
        self.hi = [k.sb(f"w_hi{i}", [P, CE], F32R) for i in range(SPLIT)]
        self.lo = [k.sb(f"w_lo{i}", [P, CE], F32R) for i in range(SPLIT)]
        self.sem = [k.sem(f"w_landed{i}") for i in range(RAW)]
        self.loaded, self.split, self.used = {}, {}, {}
        self.at = 0
        for i in range(RAW):
            self.load(i)

    def load(self, i):
        if i >= len(self.chunks):
            return
        c = self.chunks[i]
        dst = self.raw[i % RAW][:, 0:c.nk * c.nc].rearrange("p (k n) -> p k n", k=c.nk)
        self.loaded[i] = self.k.sp.load(dst, c.src, self.sem[i % RAW], i // RAW + 1,
                                        after=self.split.get(i - RAW))

    def prepare(self, i):
        if i >= len(self.chunks):
            return
        c = self.chunks[i]
        n = c.nk * c.nc
        raw, hi, lo = self.raw[i % RAW], self.hi[i % SPLIT], self.lo[i % SPLIT]
        a = self.k.act.copy(hi[:, 0:n], raw[:, 0:n], after=[self.loaded[i], self.used.get(i - SPLIT)])
        b = self.k.dve.tt(lo[:, 0:n], raw[:, 0:n], hi[:, 0:n].bitcast(F32), SUB, after=a)
        self.split[i] = [a, b]
        self.load(i + RAW)

    def next(self, chunk):
        i = self.at
        assert self.chunks[i] is chunk
        self.at += 1
        self.prepare(i + SPLIT - 1)
        view = lambda x: x[i % SPLIT][:, 0:chunk.nk * chunk.nc].rearrange("p (k n) -> p k n", k=chunk.nk)
        return i, view(self.hi), view(self.lo), self.split[i]


class Scope:
    pass


class Memory:

    def __init__(self, k):
        self.kern, self.scope = k, ExitStack()
        self.k_tok, self.v_tok = [], []
        self.k, self.v, self.f = (k.sb("mem_" + n, s, F32, self.scope)
                                  for n, s in (("k", [P, KT, T]), ("v", [P, 2, D]), ("f", [P, KT, T])))

    def prepare(self, readers):
        kern = self.kern
        t = kern.gp.load(self.f[:, :, :], kern.ap["mem_t"], kern.sem("mem_landed"), after=readers)
        yield from pause(5)
        tiles = kern.pre_norm(self.f, [t] * KT, "mem_kv_norm", self.x)
        for _ in range(KT // 2):
            tiles(2)
            yield
        self.taken = [kern.dve.last(), kern.act.last()]

    def ep_k(self, b, acc, done):
        t = self.kern.dve.tt(self.k[:, 4 * b:4 * b + 4, :], acc.rearrange("p (j t) -> p j t", j=4),
                             self.kern.rows(self.x.rms, 4), MUL, after=[done, self.x.rms.tok])
        self.k_tok.append(t)
        return t

    def ep_v(self, b, acc, done):
        t = [self.kern.act.act(self.v[:, i, 512 * b:512 * b + 512], acc[:, 512 * i:512 * i + 512], ACT.Copy,
                               scale=self.x.rms.cols[:, i:i + 1], after=[done, self.x.rms.cols_tok])
             for i in range(2)]
        self.v_tok.append(t)
        return t


class Split:

    def __init__(self, k, name, tiles, stack=None, width=T):
        self.hi = k.sb(name + "_hi", [P, tiles, width], F32R, stack)
        self.lo = k.sb(name + "_lo", [P, tiles, width], F32R, stack)
        self.tok = [None] * tiles
        self.rms_pending = False


class Kernel:
    def __init__(self, nc, ctx, ap):
        self.nc, self.ctx, self.ap = nc, ctx, ap
        self.pe = Tensor(self.sem("tensor_done"))
        self.dve = Vector(self.sem("vector_done"))
        self.act = Scalar(self.sem("scalar_done"))
        self.sp = Loads(self.sem("sync_done"))
        self.gp = Loads(self.sem("gpsimd_done"))

        acc = [ctx.enter_context(nc.psum_tensor(f"acc{i}", [P, 4 * T], F32)) for i in range(2)]
        small = [ctx.enter_context(nc.psum_tensor(f"small{i}", [P, 512], F32)) for i in range(4)]
        self.acc = Ring([b[:, :] for b in acc])
        self.small = Ring([b[:, :] for b in small])

        self.h = self.sb("h", [P, KT, T])
        self.h_tok = [None] * KT
        self.consts = self.sb("consts_sb", [P, len(CONSTS), P])
        self.params = self.sb("params_sb", [P, N_PARAMS])
        self.sq = self.sb("squares", [P, 4, T])
        self.sq_free = None
        self.rms_rows = Ring([self.sb(f"rms_rows{i}", [P, T])[:, :] for i in range(4)])
        self.rms_cols = Ring([self.sb(f"rms_cols{i}", [P, 2])[:, :] for i in range(4)])
        self.deferred = []
        self.fenced = []
        self.tmp = Ring([self.sb(f"tmp{i}", [P, 4 * T])[:, :] for i in range(2)])
        self.xn = Split(self, "xn", KT)

    def sb(self, name, shape, dtype=F32, stack=None):
        return (stack or self.ctx).enter_context(self.nc.sbuf_tensor(name, shape, dtype))

    def sem(self, name):
        return self.ctx.enter_context(self.nc.semaphore(name))

    def const(self, name):
        return self.consts[:, CONSTS.index(name), :]

    def param(self, name, i=0, n=1):
        at = PARAM_AT[name][0] + i
        return self.params[:, at:at + n]

    def fence(self):
        last = self.fenced = [q.last() for q in (self.pe, self.dve, self.act)]
        self.gp.wait(last)

        def wait():
            for q in (self.dve, self.act):
                q.wait(last)
        self.defer(FENCE_DELAY, wait)

    def defer(self, steps, fn):
        self.deferred.append([steps, fn])

    def step(self):
        for d in list(self.deferred):
            d[0] -= 1
            if d[0] <= 0:
                self.deferred.remove(d)
                d[1]()

    def spread(self, gen):
        def go():
            if next(gen, "end") != "end":
                self.defer(1, go)
        go()

    def linear(self, name, x, epilogue, tokens_out=False):
        for b, block in enumerate(self.linears[name]):
            slots = 1 + max(c.slot for c in block)
            accs = [self.acc.take() for _ in range(slots)]
            for n, chunk in enumerate(block):
                acc, free = accs[chunk.slot]
                i, w_hi, w_lo, w_tok = self.stream.next(chunk)
                for k in range(chunk.nk):
                    kk = chunk.k0 + k
                    assert x.tok[kk], "the operand is not queued yet"
                    mms = []
                    for m in range(2 if tokens_out else chunk.nc // P):
                        if tokens_out:
                            out = acc[:, 512 * m:512 * m + 512]
                            toks = slice(P * m, P * m + P)
                            terms = [(x.hi[:, kk, toks], w_hi[:, k, :]), (x.lo[:, kk, toks], w_hi[:, k, :]),
                                     (x.hi[:, kk, toks], w_lo[:, k, :])]
                            first = kk == 0
                        else:
                            tile = chunk.m0 + m
                            out = acc[:, T * tile:T * tile + T]
                            cols = slice(P * m, P * m + P)
                            terms = [(w_hi[:, k, cols], x.hi[:, kk, :]), (w_hi[:, k, cols], x.lo[:, kk, :]),
                                     (w_lo[:, k, cols], x.hi[:, kk, :])]
                            first = kk == 0 and tile % 2 == 0
                        mms += [(out, lhs, rhs, first and n == 0) for n, (lhs, rhs) in enumerate(terms)]
                    done = self.pe.group(mms, after=[w_tok, x.tok[kk], free])
                    self.stream.used[i] = done
                    self.step()
                    yield
                if all(c.slot != chunk.slot for c in block[n + 1:]):
                    finish = self.epilogue(epilogue, slots * b + chunk.slot, acc, done)
                    if x.rms_pending:
                        x.rms_pending = False
                        self.defer(EPILOGUE_DELAY, finish)
                    else:
                        finish()

    def epilogue(self, fn, n, acc, done):
        return lambda: self.acc.give(acc, fn(n, acc, done))

    def narrow(self, x, w, out):
        mms = []
        for t in range(2):
            toks = slice(P * t, P * t + P)
            for k in range(KT):
                for n, (lhs, rhs) in enumerate([(x.hi, w.hi), (x.lo, w.hi), (x.hi, w.lo)]):
                    mms.append((out[t], lhs[:, k, toks], rhs[:, k, :], t == 0 and k == 0 and n == 0))
        return mms

    def split_from(self, src, x, j, n, after):
        hi, lo = x.hi[:, j:j + n, :], x.lo[:, j:j + n, :]
        src = src.rearrange("p (j t) -> p j t", j=n)
        a = self.act.copy(hi, src, after=after)
        b = self.dve.tt(lo, src, hi.bitcast(F32), SUB, after=a)
        for i in range(j, j + n):
            x.tok[i] = b
        return b

    def squares(self, src, after, total=None):
        a = self.act.act(self.sq[:, :, :], src, ACT.Square, after=[after, self.sq_free])
        b = self.dve.tt(self.sq[:, 0:2, :], self.sq[:, 0:2, :], self.sq[:, 2:4, :], ADD, after=a)
        if total is None:
            out, free = self.rms_rows.take()
            t = self.dve.tt(out, self.sq[:, 0, :], self.sq[:, 1, :], ADD, after=[b, free])
        else:
            out = total[0]
            c = self.dve.tt(self.sq[:, 0, :], self.sq[:, 0, :], self.sq[:, 1, :], ADD, after=b)
            t = self.dve.tt(out, out, self.sq[:, 0, :], ADD, after=[c, total[1]])
        self.sq_free = t
        return out, t

    def inverse_rms(self, total, width, between=0):
        r = Scope()
        sums, tok = total
        bank, free = self.small.take()
        t = self.pe.group([(bank[:, i:i + 1], sums[:, P * i:P * i + P], self.const("ones")[:, 0:1], i == 0)
                           for i in range(2)], after=[tok, free])
        r.cols, cfree = self.rms_cols.take()
        a = self.act.act(r.cols, bank[:, 0:2], ACT.Sqrt, scale=1.0 / width, bias=self.eps[:, 0:1],
                         after=[t, cfree])
        self.small.give(bank, a)
        r.cols_tok = self.dve.recip(r.cols, r.cols, after=a)
        d = [self.dve.ts(sums[:, P * i:P * i + P], self.const("ident"), r.cols[:, i:i + 1], MUL,
                         after=[r.cols_tok, t]) for i in range(2)]
        r.rows = sums

        def rows():
            bank, free = self.small.take()
            t = self.pe.group([(bank[:, 0:T], self.const("ones"), sums, True)], after=[d, free])
            r.tok = self.act.copy(sums, bank[:, 0:T], after=t)
            self.small.give(bank, r.tok)
        if between:
            self.defer(between, rows)
        else:
            rows()
        return r

    def release(self, r):
        last = [self.dve.last(), self.act.last()]
        self.rms_rows.give(r.rows, last)
        self.rms_cols.give(r.cols, last)

    def rows(self, r, n):
        return r.rows.unsqueeze(1).to_broadcast([P, n, T])

    def pre_norm(self, src, toks, gain, x):
        total = []
        readers = []
        at = [0]

        def tiles(n=4):
            if not readers:
                readers.append(self.pe.last())
            hi = {}
            for i in range(at[0], at[0] + n):
                hi[i] = self.act.act(x.hi[:, i, :], src[:, i, :], ACT.Copy, scale=self.param(gain, i),
                                     after=[toks[i], readers])
            for i in range(at[0], at[0] + n):
                x.tok[i] = self.dve.stt(x.lo[:, i, :], src[:, i, :], self.param(gain, i),
                                        x.hi[:, i, :].bitcast(F32), MUL, SUB, after=hi[i])
            at[0] += n
            j = at[0] - 4
            if at[0] % 4 == 0:
                total.append(self.squares(src[:, j:j + 4, :], toks[j:j + 4], total[0] if total else None))
            if at[0] == KT:
                x.rms_pending = True

                def finish():
                    x.rms = self.inverse_rms(total[1], D, 2)
                self.defer(RMS_DELAY, finish)
        return tiles

    def add_normed(self, f, toks, gain, factor, then):
        total = []

        def epilogue(b, acc, done):
            total.append(self.squares(acc.rearrange("p (j t) -> p j t", j=4), done, total[0] if total else None))
            for j in range(4):
                toks[4 * b + j] = self.act.act(f[:, 4 * b + j, :], acc[:, T * j:T * j + T], ACT.Copy,
                                               scale=self.param(gain, 4 * b + j), after=done)
            return toks[4 * b + 3]

        def finish():
            r = self.inverse_rms(total[1], D)

            def scale(j):
                f2 = f[:, j:j + 2, :]
                return self.dve.tt(f2, f2, self.rows(r, 2), MUL, after=[r.tok, toks[j:j + 2]])

            t = scale(0)
            for j in range(0, KT, 2):
                h2 = self.h[:, j:j + 2, :]
                t = self.dve.stt(h2, f[:, j:j + 2, :], factor, h2, MUL, ADD, after=[t, self.h_tok[j:j + 2]])
                self.h_tok[j:j + 2] = [t, t]
                if j + 2 < KT:
                    t = scale(j + 2)
                then(2)
            self.release(r)
        return epilogue, finish

    def to_buffer(self, f, toks):
        def epilogue(b, acc, done):
            t = self.dve.copy(f[:, 4 * b:4 * b + 4, :], acc.rearrange("p (j t) -> p j t", j=4), after=done)
            toks[4 * b:4 * b + 4] = [t] * 4
            return t
        return epilogue

    def to_residual(self, factor, then):
        def epilogue(b, acc, done):
            h = self.h[:, 4 * b:4 * b + 4, :]
            t = self.dve.stt(h, acc.rearrange("p (j t) -> p j t", j=4), factor, h, MUL, ADD,
                             after=[done, self.h_tok[4 * b:4 * b + 4]])
            self.h_tok[4 * b:4 * b + 4] = [t] * 4
            then()
            return t
        return epilogue

    def ffn(self, name, then, post_gain=None):
        with ExitStack() as scope:
            hid = Split(self, name + "_hidden", FT, scope)
            f = self.sb(name + "_f", [P, KT, T], F32, scope) if post_gain else None
            f_tok = [None] * KT

            def hidden(b, acc, done):
                r = self.xn.rms
                tmp, free = self.tmp.take()
                part = lambda x, i: x[:, 512 * i:512 * i + 512].rearrange("p (j t) -> p j t", j=2)
                g = self.dve.tt(part(tmp, 0), part(acc, 0), self.rows(r, 2), MUL, after=[done, free, r.tok])
                u = self.dve.tt(part(tmp, 1), part(acc, 1), self.rows(r, 2), MUL, after=[done, free, r.tok])
                a = self.act.act(tmp[:, 0:512], tmp[:, 0:512], ACT.Silu, after=g)
                m = self.dve.tt(tmp[:, 0:512], tmp[:, 0:512], tmp[:, 512:1024], MUL, after=[a, u])
                self.tmp.give(tmp, self.split_from(tmp[:, 0:512], hid, 2 * b, 2, m))
                return [g, u]

            drain(self.linear(name + "_gate_up", self.xn, hidden))
            self.release(self.xn.rms)
            if post_gain:
                gather, finish = self.add_normed(f, f_tok, post_gain, 0.5, then)
                drain(self.linear(name + "_down", hid, gather))
                finish()
            else:
                drain(self.linear(name + "_down", hid, self.to_residual(0.5, then)))
            self.fence()

    def conv(self, taps, weight, tile0, n_tiles, src, dst, after, bias=None):
        rows = [self.act.act(dst[:, i, :], src[:, i, 0:T], ACT.Identity,
                             scale=self.param(weight, tile0 + i),
                             bias=self.param(bias, tile0 + i) if bias else 0.0, after=after)
                for i in range(4)]
        for k in range(1, taps):
            yield
            for i in range(4):
                rows[i] = self.dve.stt(dst[:, i, :], src[:, i, k:k + T],
                                       self.param(weight, n_tiles * k + tile0 + i), dst[:, i, :], MUL, ADD,
                                       after=[rows[i], after])
        return rows

    def softplus(self, parts):
        toks = []
        for x, scratch, after in parts:
            a = self.dve.ts(scratch, x, -1.0, MUL, after=after)
            toks.append(self.dve.tt(scratch, scratch, x, MIN, after=a))
        toks = [self.act.act(scratch, scratch, ACT.Exp, after=t) for (x, scratch, _), t in zip(parts, toks)]
        toks = [self.act.act(scratch, scratch, ACT.Ln, bias=self.one[:, 0:1], after=t)
                for (x, scratch, _), t in zip(parts, toks)]
        return [self.dve.stt(x, x, 0.0, scratch, MAX, ADD, after=t)
                for (x, scratch, _), t in zip(parts, toks)]

    def fox_attention(self, q, k, v, ls, tok, mixed, fox, mem):
        pe, dve, act = self.pe, self.dve, self.act
        ident = self.const("ident")
        fq, neg_ls, stat = fox.F, fox.neg_ls, fox.stat
        bufs = mem.f[:, 0:6, :].rearrange("p j t -> p (j t)").rearrange("p (h a n) -> p h a n", h=2, a=2)

        bank, free = self.small.take()
        t = pe.group([(bank[:, 0:8], self.const("tri"), ls[:, 0, :], True),
                      (bank[:, 8:16], self.const("ones"), ls[:, 0, :], False),
                      (bank[:, 8:16], self.const("tri"), ls[:, 1, :], False)], after=[tok, free])
        fq_tok = dve.copy(fq[:, :, :], bank[:, 0:16].rearrange("p (a b) -> p a b", a=2), after=t)
        self.small.give(bank, fq_tok)
        yield
        parts = [(slice(0, 128), 0), (slice(128, 384), 1)]
        tri2 = self.consts[:, 1:3, :].rearrange("p a t -> p (a t)")
        neg_free, p_free, pT_free = [None] * 2, [mem.taken] * 2, mem.taken
        soft, turned = [None] * FOX_H, [None] * FOX_H

        def scores(h):
            j, half = h // 2, h % 2
            rows = slice(FOX_D * half, FOX_D * half + FOX_D)
            neg = neg_ls[:, 2 * half:2 * half + 2, :]
            bank, free = self.small.take()
            lo, hi = bank[:, 0:128], bank[:, 128:384]
            neg_free[half] = s = pe.group([
                (lo, q[rows, j, 0:P], k[rows, j, 0:P], True),
                (lo, neg[:, 0, :], self.const("tri"), False),
                (lo, ident, self.const("neg"), False),
                (hi, q[rows, j, P:T], k[rows, j, :], True),
                (hi, neg[:, 0, :], tri2, False),
                (hi[:, P:T], neg[:, 1, :], self.const("tri"), False),
                (hi[:, P:T], ident, self.const("neg"), False)], after=[tok, neg_tok[h], free])
            p = bufs[:, half, 0, :]
            m = [dve.ts_max(p[:, c], bank[:, c], fq[:, i, h:h + 1], stat[:, h, i:i + 1],
                            after=[s, p_free[half], fq_tok]) for c, i in parts]
            self.small.give(bank, m)
            n = dve.ts(stat[:, h, 2:4], stat[:, h, 0:2], -1.0, MUL, after=m)
            soft[h] = [act.act(p[:, c], p[:, c], ACT.Exp, bias=stat[:, h, 2 + i:3 + i],
                               accum_out=stat[:, h, 4 + i:5 + i], after=n) for c, i in parts]

        def gates(h):
            if h < FOX_H:
                half = h % 2
                neg_tok[h] = dve.ts(neg_ls[:, 2 * half:2 * half + 2, :],
                                    ls[:, :, h:h + 1].to_broadcast([P, 2, P]), -1.0, MUL,
                                    after=[tok, neg_free[half]])

        def divide(h):
            p = bufs[:, h % 2, 0, :]
            r = dve.recip(stat[:, h, 4:6], stat[:, h, 4:6], after=soft[h])
            soft[h] = [dve.ts(p[:, c], p[:, c], stat[:, h, 4 + i:5 + i], MUL, after=r) for c, i in parts]

        def turn(h):
            p, pT = bufs[:, h % 2, 0, :], bufs[:, h % 2, 1, :]
            bank, free = self.small.take()
            p_free[h % 2] = t = pe.transposes([(bank[:, P * i:P * i + P], p[:, P * i:P * i + P])
                                               for i in range(3)], ident, after=[soft[h], free])
            turned[h] = act.copy(pT, bank[:, 0:384], after=[t, pT_free])
            self.small.give(bank, turned[h])

        def values(j):
            bank, free = self.small.take()
            mms = []
            for half in range(2):
                h, pT = 2 * j + half, bufs[:, half, 1, :]
                o = bank[FOX_D * half:FOX_D * half + FOX_D, 0:T]
                vh = slice(FOX_D * h, FOX_D * h + FOX_D)
                mms += [(o, v[:, 0, vh], pT[:, 0:T], True), (o[:, P:T], v[:, 1, vh], pT[:, T:384], False)]
            t = pe.group(mms, after=[turned[2 * j:2 * j + 2], free, tok])
            self.small.give(bank, self.split_from(bank[:, 0:T], mixed, j, 1, [t, self.fenced]))
            return t

        neg_tok = [None] * FOX_H
        gates(0)
        gates(1)
        yield
        for h in range(FOX_H + 2):
            if h < FOX_H:
                scores(h)
            if h % 2 and h >= 3:
                pT_free = values((h - 3) // 2)
            if h >= 1:
                gates(h + 1)
            yield
            if h < FOX_H:
                divide(h)
            if 1 <= h <= FOX_H:
                turn(h - 1)
            yield

    def gdn_prepare(self, g, c, c_tok, small_tok):
        pe, dve, act = self.pe, self.dve, self.act
        ident, ones = self.const("ident"), self.const("ones")
        H4 = GDN_H
        beta, a = g.raw[:, :, 0:4], g.raw[:, :, 4:8]
        t_beta = act.act(beta, beta, ACT.Sigmoid, after=small_tok)
        t_a = g.tok_a
        yield from pause(4)
        bank, free = self.small.take()
        mms = [(bank[:, 8 * i + 4 * m:8 * i + 4 * m + 4], self.const(n), a[:, i, :], i + m == 0)
               for i in range(2) for m, n in enumerate(("tri64", "later64"))]
        t = pe.group(mms, after=[t_a, free])
        v = bank[:, 0:16].rearrange("p (i m) -> p i m", i=2)
        t_neg = dve.ts(g.neg_cum[:, :, :], v[:, :, 0:4], -1.0, MUL, after=t)
        t1 = act.act(g.e_cum_tail[:, :, :], v, ACT.Exp, after=t_neg)
        self.small.give(bank, t1)
        t_bg = dve.tt(g.beta_ecum[:, :, :], g.e_cum_tail[:, :, 0:4], beta, MUL, after=[t1, t_beta])
        t_ab = dve.copy(g.rep[:, 0:8, :].rearrange("p (i h) t -> p i h t", i=2),
                        a.unsqueeze(3).to_broadcast([P, 2, 4, P]), after=t_a)
        t_bb = dve.copy(g.rep[:, 8:16, :].rearrange("p (i h) t -> p i h t", i=2),
                        beta.unsqueeze(3).to_broadcast([P, 2, 4, P]), after=t_beta)
        yield
        yield from until(lambda: c_tok[2])
        yield from pause(4)
        for i in range(2):
            bank, free = self.small.take()
            t = pe.transposes([(bank[:, P * h:P * h + P], c[:, 8 + h, P * i:P * i + P]) for h in range(H4)],
                              ident, after=[c_tok[2], free])
            out = [dve.ts(g.vb[:, i, h, :], bank[:, P * h:P * h + P], beta[:, i, h:h + 1], MUL,
                          after=[t, t_beta]) for h in range(H4)]
            self.small.give(bank, out)
            g.tok_vb[i] = out
            yield
        norm_tok = [None] * 8

        def square(j):
            tmp, free = self.tmp.take()
            t = act.act(tmp[:, 0:512], c[:, j:j + 2, :].rearrange("p a t -> p (a t)"), ACT.Square,
                        after=[c_tok[j // 4], free])
            return j, tmp, t

        def invert(j, tmp, t):
            bank, bfree = self.small.take()
            t = pe.group([(bank[:, n:n + 1], tmp[:, P * n:P * n + P], ones[:, 0:1], n == 0)
                          for n in range(4)], after=[t, bfree])
            cols = g.norm_cols[:, 2 * j:2 * j + 4]
            a1 = act.act(cols, bank[:, 0:4], ACT.Sqrt, bias=self.eps[:, 0:1], after=t)
            self.small.give(bank, a1)
            r = dve.recip(cols, cols, after=a1)
            return j, tmp, [dve.ts(tmp[:, 512 + P * n:640 + P * n], ident, cols[:, n:n + 1], MUL, after=r)
                            for n in range(4)]

        def scale(j, tmp, t):
            bank, bfree = self.small.take()
            t = pe.group([(bank, ones, tmp[:, 512:1024], True)], after=[t, bfree])
            dst = (g.qn if j < 4 else g.kn)[:, j % 4:j % 4 + 2, :]
            t = dve.stt(dst, c[:, j:j + 2, :], GDN_D ** -0.5 if j < 4 else 1.0,
                        bank.rearrange("p (a t) -> p a t", a=2), MUL, MUL, after=t)
            self.small.give(bank, t)
            self.tmp.give(tmp, t)
            norm_tok[j] = norm_tok[j + 1] = t

        for j in (0, 4):
            yield from until(lambda: c_tok[j // 4])
            squared = [square(j), square(j + 2)]
            yield from pause(NORM_PAUSE)
            inverted = [invert(*q) for q in squared]
            yield
            yield
            for q in inverted:
                scale(*q)
                yield
        for i in range(2):
            toks = slice(P * i, P * i + P)
            bank, free = self.small.take()
            t = pe.transposes([(bank[:, P * h:P * h + P], g.kn[:, h, toks]) for h in range(H4)], ident,
                              after=[norm_tok[4:8], free])
            out = [dve.ts(dst[:, i, h, :], bank[:, P * h:P * h + P], s[:, i, o + h:o + h + 1], MUL,
                          after=[t, t_bg])
                   for dst, s, o in ((g.kbg, g.beta_ecum, 0), (g.ktail, g.e_cum_tail, 4)) for h in range(H4)]
            self.small.give(bank, out)
            g.tok_k[i] = out
            yield
            bank, free = self.small.take()
            t = pe.group([(bank[:, P * h:P * h + P], g.rep[:, 4 * i + h, :], self.const("tri64"), True)
                          for h in range(H4)], after=[t_ab, free])
            e1 = act.act(g.e_rows[:, i, :, :].rearrange("p h t -> p (h t)"), bank, ACT.Exp, after=t)
            dec, dfree = self.tmp.take()
            e2 = [dve.ts(dec[:, P * h:P * h + P], bank[:, P * h:P * h + P], g.neg_cum[:, i, h:h + 1], ADD,
                         0.0, MIN, after=[t_neg, dfree, e1]) for h in range(H4)]
            self.small.give(bank, e2)
            e2 = act.act(dec[:, 0:512], dec[:, 0:512], ACT.Exp, after=e2)
            g.tok_rows[i] = e1
            g.tok_qd[i] = dve.tt(g.qd[:, :, toks], g.qn[:, :, toks], g.e_rows[:, i, :, :], MUL,
                                 after=[e1, norm_tok[0:4]])
            dv = dec[:, 0:512].rearrange("p (h t) -> p h t", h=H4)
            rep = lambda n: self.const(n).unsqueeze(1).to_broadcast([P, H4, P])
            t = dve.tt(dv, dv, rep("tri64"), MUL, after=e2)
            qk, free = self.small.take()
            m = pe.group([(qk[:, P * h:P * h + P], g.kn[:, h, toks], g.qn[:, h, toks], True)
                          for h in range(H4)], after=[norm_tok, free])
            t1 = dve.tt(g.attn[:, i, :, :].rearrange("p h t -> p (h t)"), qk, dec[:, 0:512], MUL, after=[t, m])
            self.small.give(qk, t1)
            g.tok_attn[i] = t1
            yield
            bb, free = self.small.take()
            m = pe.group([(bb[:, P * h:P * h + P], g.rep[:, 8 + 4 * i + h, :], ident, True)
                          for h in range(H4)], after=[t_bb, free])
            t = dve.tt(dv, dv, rep("strict64"), MUL, after=t1)
            t = dve.tt(dec[:, 0:512], dec[:, 0:512], bb, MUL, after=[t, m])
            self.small.give(bb, t)
            kk, free = self.small.take()
            m = pe.group([(kk[:, P * h:P * h + P], g.kn[:, h, toks], g.kn[:, h, toks], True)
                          for h in range(H4)], after=free)
            g.tok_L[i] = dve.tt(g.LT[:, i, :, :].rearrange("p h t -> p (h t)"), kk, dec[:, 0:512], MUL,
                                after=[t, m])
            self.small.give(kk, g.tok_L[i])
            self.tmp.give(dec, g.tok_L[i])
            yield

    def gdn_invert(self, g):
        pe, dve, act = self.pe, self.dve, self.act
        ident = self.const("ident")
        H4 = GDN_H
        rep = lambda n: self.const(n).unsqueeze(1).to_broadcast([P, H4, P])
        flat2 = lambda x, i: x[:, i, :, :].rearrange("p h t -> p (h t)")
        blk = lambda b, h: b[:, P * h:P * h + P]
        tok_x, tok_xt, n_tok, y_free, n_free = [None] * 2, [None] * 2, [None] * 2, [None] * 2, [None] * 2
        def part(b):
            for i in range(2):
                n_tok[i] = dve.tt(g.NT[:, i, :, :], g.LT[:, i, :, :], rep(f"merge{b}"), MUL,
                                  after=[g.tok_L[i], n_free[i]])

        part(1)
        for i in range(2):
            n_free[i] = tok_xt[i] = dve.tt(g.XT[:, i, :, :], rep("ident"), g.NT[:, i, :, :], SUB, after=n_tok[i])
        part(2)
        yield
        for i in range(2):
            bank, free = self.small.take()
            t = pe.transposes([(blk(bank, h), g.XT[:, i, h, :]) for h in range(H4)], ident,
                              after=[tok_xt[i], free])
            tok_x[i] = act.copy(flat2(g.X, i), bank, after=t)
            self.small.give(bank, tok_x[i])
        yield
        for b in (2, 4, 8, 16, 32):
            ys = []
            for i in range(2):
                bank, free = self.small.take()
                t = pe.group([(blk(bank, h), g.NT[:, i, h, :], g.X[:, i, h, :], True) for h in range(H4)],
                             after=[n_tok[i], tok_x[i], free])
                n_free[i] = t
                y = act.copy(flat2(g.Y, i), bank, after=[t, y_free[i]])
                self.small.give(bank, y)
                ys.append(y)
            yield
            for i in range(2):
                y = ys[i]
                banks = []
                for side in (0, 1) if b < 32 else (1,):
                    bank, free = self.small.take()
                    mms = [(blk(bank, h), g.XT[:, i, h, :], g.Y[:, i, h, :], True) if side == 0 else
                           (blk(bank, h), g.Y[:, i, h, :], g.XT[:, i, h, :], True) for h in range(H4)]
                    t = pe.group(mms, after=[y, free, tok_xt[i]])
                    banks.append((side, bank, t))
                y_free[i] = t
                for side, bank, t1 in banks:
                    x = g.X if side == 0 else g.XT
                    r = dve.tt(flat2(x, i), flat2(x, i), bank, SUB, after=[t1, t])
                    self.small.give(bank, r)
                    if side == 0:
                        tok_x[i] = r
                    else:
                        tok_xt[i] = r
            if b < 32:
                part(2 * b)
            yield
        for i in range(2):
            bank, free = self.small.take()
            t = pe.group([(blk(bank, h), g.XT[:, i, h, :], g.vb[:, i, h, :], True) for h in range(H4)],
                         after=[tok_xt[i], g.tok_vb[i], free])
            g.tok_u[i] = act.copy(flat2(g.u, i), bank, after=t)
            self.small.give(bank, g.tok_u[i])
            bank, free = self.small.take()
            t = pe.group([(blk(bank, h), g.kbg[:, i, h, :], g.XT[:, i, h, :], True) for h in range(H4)],
                         after=[tok_xt[i], g.tok_k[i], free])
            g.tok_w[i] = dve.copy(flat2(g.wT, i), bank, after=t)
            self.small.give(bank, g.tok_w[i])
            yield

    def gdn_scan(self, g, gz, gz_tok, mixed):
        pe, dve, act = self.pe, self.dve, self.act
        H4 = GDN_H
        blk = lambda b, h: b[:, P * h:P * h + P]
        s_tok, vn_free, s_free = None, None, None
        for c in range(T // CHUNK):
            i, lo = c // 2, CHUNK * (c % 2)
            rows = slice(lo, lo + CHUNK)
            cols = slice(P * i + lo, P * i + lo + CHUNK)
            if c:
                bank, free = self.small.take()
                t = pe.group([(blk(bank, h), g.wT[:, i, h, :], g.S[:, h, :], True) for h in range(H4)],
                             after=[s_tok, g.tok_w[i], free])
                vn = dve.tt(g.vn[rows, :, :].rearrange("p h e -> p (h e)"),
                            g.u[rows, i, :, :].rearrange("p h e -> p (h e)"), bank[rows, :], SUB,
                            after=[t, g.tok_u[i], vn_free])
                self.small.give(bank, vn)
            else:
                vn = dve.copy(g.vn[rows, :, :], g.u[rows, i, :, :], after=g.tok_u[i])
            yield
            if lo == 0:
                o_bank, o_free = self.small.take()
            mms = []
            for h in range(H4):
                o = o_bank[:, P * h + lo:P * h + lo + CHUNK]
                if c:
                    mms.append((o, g.S[:, h, :], g.qd[:, h, cols], True))
                mms.append((o, g.vn[rows, h, :], g.attn[rows, i, h, rows], c == 0))
            t_o = pe.group(mms, after=[vn, g.tok_qd[i], g.tok_attn[i], o_free])
            vn_free = t_o
            if c < T // CHUNK - 1:
                bank, free = self.small.take()
                t = pe.group([(blk(bank, h), g.ktail[rows, i, h, :], g.vn[rows, h, :], True)
                              for h in range(H4)], after=[free, g.tok_k[i]])
                vn_free = t
                if c:
                    s_tok = [dve.stt(g.S[:, h, :], g.S[:, h, :], g.e_rows[:, i, h, lo + 63:lo + 64],
                                     blk(bank, h), MUL, ADD, after=[t, g.tok_rows[i]]) for h in range(H4)]
                else:
                    s_tok = dve.copy(g.S[:, :, :].rearrange("p h e -> p (h e)"), bank, after=t)
                self.small.give(bank, s_tok)
            if lo:
                o3 = o_bank.rearrange("p (h t) -> p h t", h=H4)
                tmp, free = self.tmp.take()
                sq, rs = tmp[:, 0:512], tmp[:, 512:1024]
                a = act.act(sq, o_bank, ACT.Square, after=[t_o, free])
                bank, bfree = self.small.take()
                t = pe.group([(bank, self.const("ones"), sq, True)], after=[a, bfree])
                a = act.act(rs, bank, ACT.Sqrt, scale=1.0 / GDN_D, bias=self.eps[:, 0:1], after=t)
                self.small.give(bank, a)
                r = dve.recip(rs, rs, after=a)
                t = dve.stt(sq, o_bank, self.param("gdn_out_norm"), rs, MUL, MUL, after=[r])
                self.small.give(o_bank, t)
                z = gz[:, :, P * i:P * i + P]
                t = dve.tt(sq.rearrange("p (h t) -> p h t", h=H4), sq.rearrange("p (h t) -> p h t", h=H4), z,
                           MUL, after=[t, gz_tok])
                x_hi, x_lo = (x[:, 4:8, P * i:P * i + P] for x in (mixed.hi, mixed.lo))
                s3 = sq.rearrange("p (h t) -> p h t", h=H4)
                a = act.copy(x_hi, s3, after=[t, self.fenced])
                t = dve.tt(x_lo, s3, x_hi.bitcast(F32), SUB, after=a)
                self.tmp.give(tmp, t)
                mixed.tok[4:8] = [[mixed.tok[4 + n], t] for n in range(4)]
            yield

    def hybrid_mixer(self, mem):
        pe, dve, act = self.pe, self.dve, self.act
        r = self.xn
        with ExitStack() as scope:
            sb = lambda n, s, st=scope: self.sb("m1_" + n, s, F32, st)
            mem.x = Split(self, "memn", KT, scope)
            q, k = sb("fq", [P, 4, T]), sb("fk", [P, 4, T])
            v = sb("fv", [P, 2, 512])
            ls, ls_tmp = sb("ls", [P, 2, 8]), sb("ls_tmp", [P, 2, 8])
            fox, g = Scope(), Scope()
            fox.F, fox.neg_ls = sb("fox_F", [P, 2, FOX_H]), sb("fox_neg_ls", [P, 4, P])
            fox.stat = sb("fox_stat", [P, FOX_H, 6])
            g.raw, g.scratch = sb("g_raw", [P, 2, 8]), sb("g_scratch", [P, 2, 8])
            g.neg_cum, g.e_cum_tail = sb("g_neg_cum", [P, 2, 4]), sb("g_e_cum_tail", [P, 2, 8])
            g.beta_ecum, g.norm_cols = sb("g_beta_ecum", [P, 2, 4]), sb("g_norm_cols", [P, 16])
            g.S, g.vn, g.qd, gz = sb("g_S", [P, 4, P]), sb("g_vn", [P, 4, P]), sb("g_qd", [P, 4, T]), sb("gz", [P, 4, T])
            g.ktail, g.e_rows, g.attn, g.u, g.wT = (
                sb("g_" + n, [P, 2, 4, P]) for n in ("ktail", "e_rows", "attn", "u", "wT"))
            early = scope.enter_context(ExitStack())
            c = sb("conv_out", [P, 12, T], early)
            cin = sb("conv_in", [P, 4, T + 3], early)
            g.rep = mem.k[:, :, :].rearrange("p j t -> p (j t)").rearrange("p (j t) -> p j t", j=16)
            g.qn, g.kn = mem.f[:, 0:4, :], mem.f[:, 4:8, :]
            g.vb, g.kbg = (mem.v[:, i, :].rearrange("p (i h t) -> p i h t", i=2, h=4) for i in range(2))
            g.LT = g.wT
            as4 = lambda x: x.rearrange("p a t -> p (a t)").rearrange("p (i h t) -> p i h t", i=2, h=4)
            g.X, g.XT, g.Y = as4(c[:, 0:4, :]), as4(c[:, 4:8, :]), as4(c[:, 8:12, :])
            g.NT = as4(g.rep[:, 0:8, :])
            g.tok_vb, g.tok_k, g.tok_rows, g.tok_qd, g.tok_attn, g.tok_L, g.tok_u, g.tok_w = (
                [None, None] for _ in range(8))

            pad = dve.zero(cin[:, :, 0:3], self.fenced)
            tok, c_tok, gz_tok = {}, [None] * 3, []
            order = (2, 0, 1)
            state = {"cin": pad}
            four = lambda acc: acc.rearrange("p (j t) -> p j t", j=4)

            def ep_conv(n, acc, done):
                b = order[n]
                a = dve.tt(cin[:, :, 3:3 + T], four(acc), self.rows(r.rms, 4), MUL,
                           after=[done, state["cin"], r.rms.tok])
                dst = c[:, 4 * b:4 * b + 4, :]

                def steps():
                    state["cin"] = t = yield from self.conv(
                        4, "gdn_conv_w", 4 * b, 12, cin, dst, [a, pad])
                    c_tok[b] = act.act(dst, dst, ACT.Silu, after=t)
                self.spread(steps())
                return a

            def ep_q(b, acc, done):
                tok["q"] = dve.stt(q[:, :, :], four(acc), FOX_D ** -0.5, self.rows(r.rms, 4), MUL, MUL, after=done)
                return tok["q"]

            def ep_k(b, acc, done):
                tok["k"] = dve.tt(k[:, :, :], four(acc), self.rows(r.rms, 4), MUL, after=done)
                return tok["k"]

            def ep_v(b, acc, done):
                tok["v"] = [act.act(v[:, i, :], acc[:, 512 * i:512 * i + 512], ACT.Copy,
                                    scale=r.rms.cols[:, i:i + 1], after=[done, r.rms.cols_tok])
                            for i in range(2)]
                return tok["v"]

            def ep_z(b, acc, done):
                a = dve.tt(gz[:, :, :], four(acc), self.rows(r.rms, 4), MUL, after=done)
                gz_tok.append(act.act(gz[:, :, :], gz[:, :, :], ACT.Silu, after=a))
                return a

            main = one_by_one(self.linear("gdn_qkv", self.xn, ep_conv), self.linear("fox_q", self.xn, ep_q),
                              self.linear("fox_k", self.xn, ep_k),
                              self.linear("fox_v", self.xn, ep_v, tokens_out=True),
                              self.linear("gdn_z", self.xn, ep_z))
            for _ in range(KT + 1):
                next(main)
            bank, free = self.small.take()
            b3 = bank[:, 0:32].rearrange("p (i m) -> p i m", i=2)
            t = pe.group(self.narrow(self.xn, self.narrow_w["w_gates"], [b3[:, 0, :], b3[:, 1, :]]),
                         after=[free, self.narrow_tok["w_gates"], self.xn.tok])
            t = [dve.stt(out[:, i, :], b3[:, i, 8 * n:8 * n + 8], r.rms.cols[:, i:i + 1],
                         self.param("fox_f_bias", 0, 8), MUL, ADD, after=t) if n == 0 else
                 dve.ts(out[:, i, :], b3[:, i, 8 * n:8 * n + 8], r.rms.cols[:, i:i + 1], MUL, after=t)
                 for n, out in enumerate((ls, g.raw)) for i in range(2)]
            small_tok = t
            self.small.give(bank, t)
            t = dve.ts(ls[:, :, :], ls[:, :, :], -1.0, MUL, after=t)
            a = g.raw[:, :, 4:8]
            t_a = dve.tt(a, a, self.param("gdn_dt_bias", 0, 4).unsqueeze(1).to_broadcast([P, 2, 4]), ADD,
                         after=small_tok)
            ea = act.act(g.scratch[:, 0, 4:8], self.param("gdn_a_log", 0, 4), ACT.Exp, after=small_tok)
            t, t_a = self.softplus([(ls[:, :, :], ls_tmp[:, :, :], t), (a, g.scratch[:, :, 0:4], t_a)])
            tok["ls"] = dve.ts(ls[:, :, :], ls[:, :, :], -1.0, MUL, after=t)
            g.tok_a = dve.stt(a, a, -1.0, g.scratch[:, 0:1, 4:8].to_broadcast([P, 2, 4]), MUL, MUL,
                              after=[t_a, ea])

            def memory_too():
                self.spread(mem.prepare([pe.last(), dve.last(), act.last()]))
                yield

            weave(main, one_by_one(self.gdn_prepare(g, c, c_tok, small_tok), memory_too(), self.gdn_invert(g)))
            self.release(self.xn.rms)
            early.close()
            self.fence()
            late = scope.enter_context(ExitStack())
            mixed = Split(self, "mixed", KT, late)

            attention = self.fox_attention(q, k, v, ls, [tok[n] for n in ("q", "k", "v", "ls")], mixed, fox, mem)
            weave(one_by_one(self.linear("mem_k", mem.x, mem.ep_k),
                             self.linear("mem_v0", mem.x, mem.ep_v, tokens_out=True)),
                  in_turn(attention, self.gdn_scan(g, gz, gz_tok, mixed)))

            f, f_tok = mem.f, [None] * KT
            pre = self.pre_norm(self.h, self.h_tok, "mem_pre_norm", self.xn)
            gather, finish = self.add_normed(f, f_tok, "mix_post_norm", 1.0, pre)
            drain(self.linear("w_out", mixed, gather))
            self.defer(4, finish)
            drain(self.linear("mem_v1", mem.x, lambda b, acc, done: mem.ep_v(1, acc, done), tokens_out=True))

    def memory_attention(self, mem, then):
        pe, dve, act = self.pe, self.dve, self.act
        ident = self.const("ident")
        with ExitStack() as scope:
            sb = lambda n, s: self.sb("mem_" + n, s, F32, scope)
            k, v, q = mem.k, mem.v, sb("q", [P, KT, T])
            o = Split(self, "mem_o", KT, scope)
            f, f_tok = mem.f, [None] * KT
            bufs = Ring([sb(f"p{i}", [P, 2, 512]) for i in range(2)])
            stat = sb("stat", [P, MEM_H, 6])
            q_tok = [None, None]

            def ep_q(b, acc, done):
                q_tok[b] = dve.stt(q[:, 4 * b:4 * b + 4, :], acc.rearrange("p (j t) -> p j t", j=4),
                                   MEM_D ** -0.5, self.rows(self.xn.rms, 4), MUL, MUL,
                                   after=[done, self.xn.rms.tok])
                return q_tok[b]

            def head(h):
                bank, free = self.small.take()
                s = pe.group([(bank[:, T * i:T * i + T], q[:, 2 * h + d, P * i:P * i + P], k[:, 2 * h + d, :],
                               d == 0) for i in range(2) for d in range(2)],
                             after=[q_tok[h // 2], mem.k_tok, free])
                buf, free = bufs.take()
                p, pT = buf[:, 0, :], buf[:, 1, :]
                m = dve.rmax(stat[:, h, 0:2], bank.rearrange("p (i m) -> p i m", i=2), after=s)
                n = dve.ts(stat[:, h, 2:4], stat[:, h, 0:2], -1.0, MUL, after=m)
                e = [act.act(p[:, T * i:T * i + T], bank[:, T * i:T * i + T], ACT.Exp,
                             bias=stat[:, h, 2 + i:3 + i], accum_out=stat[:, h, 4 + i:5 + i],
                             after=[n, free]) for i in range(2)]
                self.small.give(bank, e)
                r = dve.recip(stat[:, h, 4:6], stat[:, h, 4:6], after=e)
                d = [dve.ts(p[:, T * i:T * i + T], p[:, T * i:T * i + T], stat[:, h, 4 + i:5 + i], MUL,
                            after=r) for i in range(2)]
                yield
                bank, free = self.small.take()
                t = pe.transposes([(bank[:, T * mt + P * i:T * mt + P * i + P],
                                    p[:, T * i + P * mt:T * i + P * mt + P])
                                   for mt in range(2) for i in range(2)], ident, after=[d, free])
                c = act.copy(pT, bank, after=t)
                self.small.give(bank, c)
                yield
                bank, free = self.small.take()
                t = pe.group([(bank[:, T * d:T * d + T],
                               v[:, mt, MEM_D * h + P * d:MEM_D * h + P * d + P],
                               pT[:, T * mt:T * mt + T], mt == 0) for d in range(2) for mt in range(2)],
                             after=[c, free, mem.v_tok])
                bufs.give(buf, t)
                self.small.give(bank, self.split_from(bank, o, 2 * h, 2, t))
                yield

            weave(self.linear("mem_q", self.xn, ep_q), in_turn(head(0), head(1)), start=KT + EPILOGUE_DELAY)
            self.release(self.xn.rms)
            gather, finish = self.add_normed(f, f_tok, "mem_post_norm", 1.0, then)
            weave(self.linear("mem_o", o, gather), in_turn(head(2), head(3)))
            finish()
        mem.scope.close()
        self.fence()

    def ssd(self, L, s, scope):
        pe, dve, act = self.pe, self.dve, self.act
        ident = self.const("ident")
        blk = lambda b, h: b[:, P * h:P * h + P]
        HG = SSM_H // SSM_G
        dt, a = s.dt, s.a
        bank, free = self.small.take()
        t = pe.group([(bank[:, 0:32], self.const("tri"), a[:, 0, :], True),
                      (bank[:, 32:64], self.const("tri"), a[:, 1, :], True),
                      (bank[:, 64:96], self.const("later"), a[:, 0, :], True)], after=[s.a_tok, free])
        t_neg = dve.ts(s.neg_cum[:, :, :].rearrange("p i h -> p (i h)"), bank[:, 0:64], -1.0, MUL, after=t)
        t_end = act.act(s.to_end[:, :], bank[:, 64:96], ACT.Exp, after=t_neg)
        self.small.give(bank, t_end)
        yield
        bank, free = self.small.take()
        t = pe.transposes([(blk(bank, g), s.bc[:, g, 0:P]) for g in range(SSM_G)], ident,
                          after=[s.bc_tok, free])
        b_tok = act.copy(s.b_rows[:, :, :].rearrange("p g n -> p (g n)"), bank, after=t)
        self.small.give(bank, b_tok)
        yield
        x_tok = {}
        for g in range(SSM_G):
            for i in range(2):
                bank, free = self.small.take()
                t = pe.transposes([(blk(bank, j), s.x[:, 4 * g + j, P * i:P * i + P]) for j in range(4)], ident,
                                  after=[s.x_tok[g], free])
                x_tok[i, g] = dve.tt(
                    s.xdt[:, i, 512 * g:512 * g + 512].rearrange("p (h d) -> p h d", h=HG),
                    bank.rearrange("p (h d) -> p h d", h=HG),
                    dt[:, i, HG * g:HG * g + HG].unsqueeze(2).to_broadcast([P, HG, SSM_P]), MUL,
                    after=[t, s.dt_tok])
                self.small.give(bank, x_tok[i, g])
                yield
        free = Scope()
        free.rep, free.state, free.xe, free.cb = [None, None], [None, None], None, [None, None]
        xe_tok, st_tok, cb_tok, r_tok = {}, {}, {}, {}
        stages = [(g, i, half) for g in range(SSM_G) for i in range(2) for half in range(2)]

        def scale_x(g):
            xe_tok[g] = dve.tt(s.xe[:, :].rearrange("p (h d) -> p h d", h=HG),
                               s.xdt[:, 0, 512 * g:512 * g + 512].rearrange("p (h d) -> p h d", h=HG),
                               s.to_end[:, HG * g:HG * g + HG].unsqueeze(2).to_broadcast([P, HG, SSM_P]), MUL,
                               after=[t_end, x_tok[0, g], free.xe])

        def state_of(g):
            bank, bfree = self.small.take()
            free.xe = t = pe.group([(bank, s.b_rows[:, g, :], s.xe[:, :], True)], after=[xe_tok[g], b_tok, bfree])
            st_tok[g] = act.copy(s.state[g % 2], bank, after=[t, free.state[g % 2]])
            self.small.give(bank, st_tok[g])

        def repeat(n):
            if n < len(stages):
                g, i, half = stages[n]
                h0 = HG * g + 4 * half
                r_tok[n] = act.copy(s.rep[:, n % 2, :, :],
                                    a[:, i, h0:h0 + 4].unsqueeze(2).to_broadcast([P, 4, P]),
                                    after=[s.a_tok, free.rep[n % 2]])

        def products(g, i):
            toks = slice(P * i, P * i + P)
            bank, bfree = self.small.take()
            t = pe.group([(bank[:, 0:P], s.bc[:, g, toks], s.bc[:, 4 + g, toks], True)], after=bfree)
            cb_tok[g, i] = dve.tt(s.cb[i], bank[:, 0:P], self.const("tri"), MUL, after=[t, free.cb[i]])
            self.small.give(bank, cb_tok[g, i])

        repeat(0)
        repeat(1)
        scale_x(0)
        yield
        products(0, 0)
        yield from pause(3)
        late = None
        for n, (g, i, half) in enumerate(stages):
            st = Scope()
            st.n, st.g, st.i, st.half, st.h0 = n, g, i, half, HG * g + 4 * half
            self.ssd_decay(s, st, free, [r_tok[n], t_neg])
            repeat(n + 2)
            if i == 0 and half == 1:
                state_of(g)
            yield
            self.ssd_mask(s, st, free, cb_tok[g, i])
            if late:
                self.ssd_output(L, s, late, free, [x_tok[late.i, late.g], st_tok[late.g] if late.i else None])
            late = st
            if half == 1 and n + 1 < len(stages):
                products(*stages[n + 1][0:2])
            if half == 1 and i == 1 and g + 1 < SSM_G:
                scale_x(g + 1)
            if half == 1:
                yield from pause(2)
            yield
        self.ssd_output(L, s, late, free, [x_tok[late.i, late.g], st_tok[late.g]])
        yield

    def ssd_decay(self, s, st, free, ready):
        pe, dve, act = self.pe, self.dve, self.act
        blk = lambda b, h: b[:, P * h:P * h + P]
        bank, bfree = self.small.take()
        free.rep[st.n % 2] = t = pe.group([(blk(bank, n), s.rep[:, st.n % 2, n, :], self.const("tri"), True)
                                 for n in range(4)], after=[ready, bfree])
        st.m, mfree = s.m.take()
        d_tok = [dve.ts(blk(st.m, n), blk(bank, n), s.neg_cum[:, st.i, st.h0 + n:st.h0 + n + 1], ADD, 0.0, MIN,
                        after=[t, mfree, ready]) for n in range(4)]
        st.e_tok = act.act(st.m[:, :], st.m[:, :], ACT.Exp, after=d_tok)
        st.ep = st.ep_tok = None
        if st.i == 1:
            st.ep, epfree = s.e_pair.take()
            b4 = bank.rearrange("p (n t) -> p n t", n=4)
            st.ep_tok = [act.act(st.ep[64 * r:64 * r + 64, :, :], b4[64 * r:64 * r + 64, r:4:2, :],
                                 ACT.Exp, after=[d_tok, epfree]) for r in range(2)]
        self.small.give(bank, [d_tok, st.ep_tok])

    def ssd_mask(self, s, st, free, cb_tok):
        m3 = st.m[:, :].rearrange("p (n t) -> p n t", n=4)
        free.cb[st.i] = st.m_tok = self.dve.tt(m3, m3, s.cb[st.i].unsqueeze(1).to_broadcast([P, 4, P]), MUL,
                                               after=[st.e_tok, cb_tok])

    def ssd_output(self, L, s, st, free, ready):
        pe, dve = self.pe, self.dve
        g, i, half, m, ep = st.g, st.i, st.half, st.m, st.ep
        toks = slice(P * i, P * i + P)
        j = st.h0 // 2
        yb, bfree = self.small.take()
        mms = []
        for n in range(4):
            h = st.h0 + n
            o = yb[64 * (n % 2):64 * (n % 2) + 64, P * (n // 2):P * (n // 2) + P]
            mms.append((o, s.xdt[:, i, 64 * h:64 * h + 64], m[:, P * n:P * n + P], True))
        if i == 1:
            mms += [(yb[:, T + P * n:T + P * n + P],
                     s.state[g % 2][:, P * (2 * half + n):P * (2 * half + n) + P],
                     s.bc[:, 4 + g, toks], True) for n in range(2)]
        t = pe.group(mms, after=[st.m_tok, bfree, ready])
        s.m.give(m, t)
        free.state[g % 2] = t
        if i == 1:
            pair = lambda x: x.rearrange("p (n t) -> p n t", n=2)
            t = dve.tt(ep[:, :, :], ep[:, :, :], pair(yb[:, T:2 * T]), MUL, after=[t, st.ep_tok])
            t = dve.tt(ep[:, :, :], ep[:, :, :], pair(yb[:, 0:T]), ADD, after=t)
            self.small.give(yb, t)
            src = [ep[:, n, :] for n in range(2)]
        else:
            src = [yb[:, P * n:P * n + P] for n in range(2)]
        y = [dve.stt(s.x[:, j + n, toks], s.x[:, j + n, toks], self.param(f"m_D_2{L}", j + n), src[n],
                     MUL, ADD, after=t) for n in range(2)]
        if i == 1:
            s.e_pair.give(ep, y)
        else:
            self.small.give(yb, y)
        for n in range(2):
            s.y_tok[j + n].append(y[n])

    def hybrid_mixer_2(self, L, then):
        pe, dve, act = self.pe, self.dve, self.act
        with ExitStack() as outer:
            osb = lambda n, s: self.sb(f"m2{L}_" + n, s, F32, outer)
            s = Scope()
            s.x, s.bc = osb("x", [P, 16, T]), osb("bc", [P, 8, T])
            cx, sgm = osb("cx", [P, 8, T + 2]), osb("gate_m", [P, 8, T])
            ya = cx[:, :, 0:T]
            s.x_tok, s.y_tok = [None] * 4, [[] for _ in range(16)]
            inner = outer.enter_context(ExitStack())
            sb = lambda n, s_, d=F32: self.sb(f"m2{L}_" + n, s_, d, inner)
            cin = sb("conv_in", [P, 4, T + 3])
            s.dt, s.a, s.neg_cum = (sb(n, [P, 2, SSM_H]) for n in ("dt", "a", "neg_cum"))
            s.dt_tmp, s.to_end, s.e_a = sb("dt_tmp", [P, 2, SSM_H]), sb("to_end", [P, SSM_H]), sb("e_a", [P, SSM_H])
            s.b_rows, s.xdt = sb("b_rows", [P, 4, P]), sb("xdt", [P, 2, 2048])
            s.xe = sb("xe", [P, 512])
            s.state = [sb(f"state{i}", [P, 512])[:, :] for i in range(2)]
            s.cb = [sb(f"cb{i}", [P, P])[:, :] for i in range(2)]
            s.rep = sb("rep", [P, 2, 4, P])
            s.m = Ring([sb(f"decay{i}", [P, 512]) for i in range(2)])
            s.e_pair = Ring([sb(f"e_pair{i}", [P, 2, P]) for i in range(2)])
            yain = Split(self, f"m2{L}_sc_in", KT, inner)
            xn = self.xn
            four = lambda acc: acc.rearrange("p (j t) -> p j t", j=4)

            pad = [dve.zero(cin[:, :, 0:3], self.fenced), dve.zero(cx[:, :, 0:2])]
            ea = act.act(s.e_a[:, :], self.param(f"m_A_log_2{L}", 0, 32), ACT.Exp, self.fenced)
            state = {"cin": pad}
            cx_tok = [None, None]

            def ep_xbc(b, acc, done):
                a = dve.tt(cin[:, :, 3:3 + T], four(acc), self.rows(xn.rms, 4), MUL,
                           after=[done, state["cin"], xn.rms.tok])
                dst = s.x[:, 4 * b:4 * b + 4, :] if b < 4 else s.bc[:, 4 * b - 16:4 * b - 12, :]

                def steps():
                    state["cin"] = t = yield from self.conv(
                        4, f"m_conv_w_2{L}", 4 * b, 24, cin, dst, [a, pad], bias=f"m_conv_b_2{L}")
                    r = act.act(dst, dst, ACT.Silu, after=t)
                    if b < 4:
                        s.x_tok[b] = r
                    else:
                        s.bc_tok[b - 4] = r
                self.spread(steps())
                return a

            def ep_first(n, acc, done):
                kind, b = FIRST_BLOCKS[n]
                if kind == "xbc":
                    return ep_xbc(b, acc, done)
                view = cx[:, 4 * b:4 * b + 4, 2:2 + T]
                if kind == "c":
                    cx_tok[b] = t = dve.tt(view, four(acc), self.rows(xn.rms, 4), MUL,
                                           after=[done, pad, xn.rms.tok])
                else:
                    t = dve.tt(view, view, self.rows(xn.rms, 4), MUL, after=cx_tok[b])
                    cx_tok[b] = t = dve.tt(view, view, four(acc), MUL, after=[done, t])
                return t

            s.bc_tok = [None, None]
            first = self.linear(f"first{L}", xn, ep_first)
            for _ in range(KT + 1):
                next(first)
            bank, free = self.small.take()
            b3 = bank[:, 0:64].rearrange("p (i m) -> p i m", i=2)
            w = self.narrow_w[f"w_dt{L}"]
            t = pe.group(self.narrow(xn, w, [b3[:, 0, :], b3[:, 1, :]]),
                         after=[free, self.narrow_tok[f"w_dt{L}"], xn.tok])
            rep2 = lambda x: x.unsqueeze(1).to_broadcast([P, 2, SSM_H])
            t = [dve.stt(s.dt[:, i, :], b3[:, i, :], xn.rms.cols[:, i:i + 1],
                         self.param(f"m_dt_bias_2{L}", 0, 32), MUL, ADD, after=[t, xn.rms.cols_tok])
                 for i in range(2)]
            self.small.give(bank, t)
            s.dt_tok = self.softplus([(s.dt[:, :, :], s.dt_tmp[:, :, :], t)])
            s.a_tok = dve.stt(s.a[:, :, :], s.dt[:, :, :], -1.0, rep2(s.e_a[:, :]), MUL, MUL,
                              after=[s.dt_tok, ea])
            scan = self.ssd(L, s, inner)
            for n, _ in enumerate(first, KT + 1):
                if n in SCAN_AHEAD:
                    next(scan)

            ya_tok, sgm_tok = [None, None], [None, None]

            short = [None, None]

            def short_conv():
                for n in range(2):
                    tmp, free = self.tmp.take()
                    t = yield from self.conv(3, f"sc_conv_w_2{L}", 4 * n, 8, cx[:, 4 * n:4 * n + 4, :],
                                             four(tmp), [cx_tok[n], free, pad])
                    cx_tok[n] = t
                    yield
                    short[n] = tmp, dve.tt(four(tmp), four(tmp), self.rows(xn.rms, 4), MUL, after=t)
                    yield

            def ep_sc_b(n, acc, done):
                tmp, tok = short[n]
                t = dve.tt(four(tmp), four(tmp), four(acc), MUL, after=[tok, done])
                self.tmp.give(tmp, self.split_from(tmp, yain, 4 * n, 4, t))
                return t

            def gate(out, toks, readers):
                def epilogue(b, acc, done):
                    v = out[:, 4 * b:4 * b + 4, :]
                    t = dve.tt(v, four(acc), self.rows(xn.rms, 4), MUL, after=[done, readers])
                    toks[b] = act.act(v, v, ACT.Sigmoid, after=t)
                    return t
                return epilogue

            def ep_ya(b, acc, done):
                v = ya[:, 4 * b:4 * b + 4, :]
                ya_tok[b] = dve.tt(v, v, four(acc), MUL, after=[done, ya_tok[b]])
                return ya_tok[b]

            self.spread(apart(short_conv(), 2))
            weave(one_by_one(self.linear(f"gate_m{L}", xn, gate(sgm, sgm_tok, None)),
                             self.linear(f"sc_b{L}", xn, ep_sc_b),
                             self.linear(f"gate_a{L}", xn, gate(ya, ya_tok, cx_tok)),
                             self.linear(f"sc_out{L}", yain, ep_ya)),
                  scan, start=8)
            inner.close()
            reuse = [pe.last(), dve.last(), act.last()]
            yn = Split(self, f"m2{L}_yn", 16, outer)
            merged = Split(self, f"m2{L}_merged", KT, outer)
            busy = []

            def ep_z(b, acc, done):
                y = s.x[:, 4 * b:4 * b + 4, :]
                tmp, free = self.tmp.take()
                a = dve.tt(four(tmp), four(acc), self.rows(xn.rms, 4), MUL, after=[done, free])
                t = act.act(tmp, tmp, ACT.Silu, after=a)
                t = dve.tt(y, y, four(tmp), MUL, after=[t, s.y_tok[4 * b:4 * b + 4]])
                self.tmp.give(tmp, t)
                total = self.squares(y, t)

                def finish():
                    r = self.inverse_rms(total, 512, 2)
                    self.defer(3, lambda: scale(r))

                def scale(r):
                    for j in range(4 * b, 4 * b + 4, 2):
                        tmp, free = self.tmp.take()
                        for i in range(2):
                            t = dve.stt(tmp[:, T * i:T * i + T], s.x[:, j + i, :],
                                        self.param(f"m_norm_2{L}", j + i), r.rows, MUL, MUL, after=[r.tok, free])
                        self.tmp.give(tmp, self.split_from(tmp[:, 0:2 * T], yn, j, 2, [t, reuse]))
                    self.release(r)
                self.defer(7, finish)
                return a

            drain(self.linear(f"z{L}", xn, ep_z))
            self.release(xn.rms)

            def ep_merge(b, acc, done):
                v, u = sgm[:, 4 * b:4 * b + 4, :], ya[:, 4 * b:4 * b + 4, :]
                t0 = t = dve.tt(v, v, four(acc), MUL, after=[done, sgm_tok[b]])
                t = dve.tt(v, v, u, ADD, after=[t, ya_tok[b]])
                self.split_from(v.rearrange("p j t -> p (j t)"), merged, 4 * b, 4, [t, reuse])
                return t0

            drain(self.linear(f"m_out{L}", yn, ep_merge))
            drain(self.linear(f"w_o{L}", merged, self.to_residual(1.0, then)))
            self.fence()

    def ple_prepare(self, L, scope):
        s = Scope()
        p_in = self.sb(f"ple{L}_p", [P, 2, T], F32, scope)
        s.px = Split(self, f"ple{L}_px", 2, scope)
        s.xn = Split(self, f"ple{L}_xn", KT, scope)
        s.proj = self.sb(f"ple{L}_proj", [P, KT, T], F32, scope)
        s.gate = self.sb(f"ple{L}_gate", [P, KT, T], F32, scope)
        t = self.gp.load(p_in[:, :, :], self.ap["p_t"][L], self.sem(f"p_landed{L}"))
        self.defer(FENCE_DELAY + 4,
                   lambda: self.split_from(p_in[:, :, :].rearrange("p a t -> p (a t)"), s.px, 0, 2, t))
        return s

    def ple(self, L, s, then):
        dve, act = self.dve, self.act
        with ExitStack() as scope:
            px, xn, proj, gate = s.px, s.xn, s.proj, s.gate
            proj_tok = [None] * KT

            def ep(b, acc, done):
                halves = [slice(4 * b + n, 4 * b + n + 2) for n in (0, 2)]
                rows = self.rows(xn.rms, 2)
                read = [dve.tt(gate[:, sl, :], acc[:, T * n:T * n + 2 * T].rearrange("p (j t) -> p j t", j=2),
                               rows, MUL, after=[done, xn.rms.tok]) for n, sl in zip((0, 2), halves)]
                toks = [act.act(gate[:, sl, :], gate[:, sl, :], ACT.Sigmoid, after=t)
                        for sl, t in zip(halves, read)]
                for sl, t in zip(halves, toks):
                    t = dve.tt(gate[:, sl, :], gate[:, sl, :], proj[:, sl, :], MUL, after=[t, proj_tok[sl]])
                    t = dve.tt(self.h[:, sl, :], self.h[:, sl, :], gate[:, sl, :], ADD,
                               after=[t, self.h_tok[sl]])
                    self.h_tok[sl] = [t] * 2
                then()
                return read

            drain(self.linear(f"ple_proj{L}", px, self.to_buffer(proj, proj_tok)))
            drain(self.linear(f"ple_gate{L}", xn, ep))
            self.release(xn.rms)
            self.fence()

    def program(self):
        A = self.ap
        W1, pe, dve, act = A["w_in"][0], self.pe, self.dve, self.act
        L = {}
        L["f1_gate_up"] = gate_up_blocks(A["ffn1_w_gate"][0], A["ffn1_w_up"][0])
        L["f1_down"] = column_blocks(A["ffn1_w_down"][0], 0, D)
        L["gdn_qkv"] = [column_blocks(W1, 1544 + 512 * b, 2056 + 512 * b)[0] for b in (2, 0, 1)]
        L["fox_q"] = column_blocks(W1, 0, 512)
        L["fox_k"] = column_blocks(W1, 512, 1024)
        L["fox_v"] = column_blocks(W1, 1024, 1536)
        L["gdn_z"] = column_blocks(W1, 3080, 3592)
        L["mem_k"] = column_blocks(A["mem_w_kv"][0], 0, D)
        L["mem_v0"] = column_blocks(A["mem_w_kv"][0], D, D + 512)
        L["w_out"] = halved_block(A["w_out"][0])
        L["mem_v1"] = column_blocks(A["mem_w_kv"][0], D + 512, 2 * D)
        L["mem_q"] = column_blocks(A["mem_w_q"][0], 0, D)
        L["mem_o"] = halved_block(A["mem_w_o"][0])
        L["f2_gate_up"] = gate_up_blocks(A["ffn2_w_gate"][0], A["ffn2_w_up"][0])
        L["f2_down"] = column_blocks(A["ffn2_w_down"][0], 0, D)
        for i in range(DEPTH_2):
            w = A["w_in_2"][i]
            L[f"g1{i}_gate_up"] = gate_up_blocks(A["ffn1_wg_2"][i], A["ffn1_wu_2"][i])
            L[f"g1{i}_down"] = column_blocks(A["ffn1_wd_2"][i], 0, D)
            at = {"xbc": 5120, "c": 1024, "x": 2048}
            L[f"first{i}"] = [column_blocks(w, at[n] + 512 * b, at[n] + 512 * b + 512)[0]
                              for n, b in FIRST_BLOCKS]
            L[f"gate_m{i}"] = column_blocks(w, 9248, 10272)
            L[f"sc_b{i}"] = column_blocks(w, 0, 1024)
            L[f"gate_a{i}"] = column_blocks(w, 8224, 9248)
            L[f"sc_out{i}"] = column_blocks(A["sc_w_out_2"][i], 0, D)
            L[f"z{i}"] = column_blocks(w, 3072, 5120)
            L[f"m_out{i}"] = column_blocks(A["m_w_out_2"][i], 0, D)
            L[f"w_o{i}"] = halved_block(A["w_o_2"][i])
            L[f"g2{i}_gate_up"] = gate_up_blocks(A["ffn2_wg_2"][i], A["ffn2_wu_2"][i])
            L[f"g2{i}_down"] = column_blocks(A["ffn2_wd_2"][i], 0, D)
            L[f"ple_proj{i}"] = column_blocks(A["ple_w_proj_2"][i], 0, D)
            L[f"ple_gate{i}"] = column_blocks(A["ple_w_gate_2"][i], 0, D)
        self.linears = L

        params_tok = self.sp.load(self.params[:, :], A["params"], self.sem("params_landed"))
        for n in range(2):
            t = self.sp.load(self.h[:, 4 * n:4 * n + 4, :], A["x_t"][:, 4 * n:4 * n + 4, :], self.sem(f"x_landed{n}"))
            self.h_tok[4 * n:4 * n + 4] = [t] * 4
        consts_tok = self.gp.load(self.consts[:, :, :], A["consts"], self.sem("consts_landed"))
        for q in (dve, act):
            q.wait(params_tok)
        self.eps, self.one = self.sb("eps", [P, 1]), self.sb("one", [P, 1])
        t0 = dve.run(lambda e: e.memset(self.eps[:, :], EPS))
        t1 = dve.run(lambda e: e.memset(self.one[:, :], 1.0))
        act.wait(t0, t1)

        self.stream = Stream(self, [c for blocks in L.values() for b in blocks for c in b])
        splits = {n: Split(self, n, KT, width=w)
                  for n, w in (("w_gates", 16), ("w_dt0", SSM_H), ("w_dt1", SSM_H))}
        loading = ExitStack()
        self.narrow_w, self.narrow_tok = splits, {}

        def narrow_weights(name, parts, n):
            raw = self.sb(name + "_raw", [P, KT, n], F32, loading)
            w = splits[name]
            at, toks = 0, []
            for part in parts:
                m = part.shape[1]
                toks.append(self.gp.load(raw[:, :, at:at + m], part.rearrange("(k p) n -> p k n", p=P),
                                         self.sem(f"{name}_landed{at}")))
                at += m

            def split():
                a = act.copy(w.hi[:, :, :], raw[:, :, :], after=toks)
                self.narrow_tok[name] = dve.tt(w.lo[:, :, :], raw[:, :, :], w.hi[:, :, :].bitcast(F32), SUB,
                                               after=a)
            self.defer(20, split)

        narrow_weights("w_gates", [W1[:, 1536:1544], W1[:, 3592:3600]], 16)
        for i in range(DEPTH_2):
            narrow_weights(f"w_dt{i}", [A["w_in_2"][i][:, 8192:8224]], SSM_H)

        def pre(gain):
            return self.pre_norm(self.h, self.h_tok, gain, self.xn)

        start = pre("ffn1_pre_norm")
        start()
        start()
        for i in range(SPLIT - 1):
            self.stream.prepare(i)
        self.defer(RMS_DELAY - 1, lambda: [q.wait(consts_tok) for q in (pe, dve, act)])
        self.ffn("f1", pre("mix_pre_norm"), "ffn1_post_norm")
        loading.close()
        mem = Memory(self)
        self.hybrid_mixer(mem)
        self.memory_attention(mem, pre("ffn2_pre_norm"))
        self.ffn("f2", pre("ffn1_norm_20"), "ffn2_post_norm")
        final = []

        def last():
            j = 4 * len(final)
            final.append(self.squares(self.h[:, j:j + 4, :], self.h_tok[j:j + 4], final[0] if final else None))

        for i in range(DEPTH_2):
            self.ffn(f"g1{i}", pre(f"mix_norm_2{i}"))
            self.hybrid_mixer_2(i, pre(f"ffn2_norm_2{i}"))
            with ExitStack() as scope:
                s = self.ple_prepare(i, scope)
                self.ffn(f"g2{i}", self.pre_norm(self.h, self.h_tok, f"ple_norm_2{i}", s.xn))
                self.ple(i, s, pre("ffn1_norm_21") if i == 0 else last)

        r = self.inverse_rms(final[1], D)
        stored = []
        for n in range(2):
            done = [dve.stt(self.h[:, j, :], self.h[:, j, :], self.param("final_norm_2", j), r.rows,
                            MUL, MUL, after=[r.tok, self.h_tok[j]]) for j in range(4 * n, 4 * n + 4)]
            stored.append(self.sp.load(A["out"][:, 4 * n:4 * n + 4, :], self.h[:, 4 * n:4 * n + 4, :],
                                       self.sem(f"out_stored{n}"), after=done))
        self.sp.wait(stored)


def build(nc, ap):
    with ExitStack() as ctx:
        k = Kernel(nc, ctx, ap)
        k.program()
        block = ctx.enter_context(nc.Block())
        for queue, place in ((k.sp, block.sync), (k.gp, block.gpsimd), (k.pe, block.tensor),
                             (k.dve, block.vector), (k.act, block.scalar)):
            def body(e, queue=queue):
                for op in queue.ops:
                    op(e)
            place(body)


WEIGHTS = ["ffn1_w_gate", "ffn1_w_up", "ffn1_w_down", "w_in", "w_out", "mem_w_q", "mem_w_kv", "mem_w_o",
           "ffn2_w_gate", "ffn2_w_up", "ffn2_w_down", "ffn1_wg_2", "ffn1_wu_2", "ffn1_wd_2", "w_in_2",
           "sc_w_out_2", "m_w_out_2", "w_o_2", "ffn2_wg_2", "ffn2_wu_2", "ffn2_wd_2", "ple_w_gate_2",
           "ple_w_proj_2"]


def kernel(**inputs):
    import concourse.bacc as bacc
    from concourse.bass_utils import run_bass_kernel_spmd

    x = {n: np.asarray(a) for n, a in inputs.items()}

    def feature_major(a):
        return np.ascontiguousarray(a.T.reshape(-1, P, a.shape[0]).transpose(1, 0, 2))

    def columns(a):
        return a.reshape(-1, P).T

    rows = ("fox_f_bias", "gdn_a_log", "gdn_dt_bias", "m_dt_bias_2", "m_A_log_2")
    cols = []
    for name, n in PARAMS:
        base, layer = (name[:-1], int(name[-1])) if name not in x else (name, 0)
        a = x[base] if name == "final_norm_2" else x[base][layer]
        if base in rows:
            a = np.broadcast_to(a[None, :], (P, n))
        elif base == "m_D_2":
            a = columns(np.repeat(a, SSM_P))
        else:
            a = columns(a)
        assert a.shape == (P, n), name
        cols.append(a)
    arrays = {n: np.ascontiguousarray(x[n]) for n in WEIGHTS}
    arrays["params"] = np.ascontiguousarray(np.concatenate(cols, axis=1))
    arrays["consts"] = constant_matrices()
    arrays["x_t"] = feature_major(x["x"][0])
    arrays["mem_t"] = feature_major(x["mem"][0])
    arrays["p_t"] = np.stack([feature_major(x["p_2"][i, 0]) for i in range(DEPTH_2)])

    nc = bacc.Bacc("TRN2", target_bir_lowering=False, num_devices=1)
    ap = {n: nc.dram_tensor(n + "_dram", a.shape, F32, kind="ExternalInput").ap() for n, a in arrays.items()}
    ap["out"] = nc.dram_tensor("out_dram", (P, KT, T), F32, kind="ExternalOutput").ap()
    build(nc, ap)
    r = run_bass_kernel_spmd(nc, [{n + "_dram": a for n, a in arrays.items()}], core_ids=[0])
    out = r.results[0]["out_dram"]
    return np.ascontiguousarray(out.transpose(1, 0, 2).reshape(D, T).T)[None]
```
